# Optimizing a Trainium2 kernel written in Bass

```python
import math
import jax, jax.numpy as jnp
from jax import lax
import numpy as np

D_MODEL = 1024
BATCH = 1
SEQ = 1024
DEPTH = 1
DEC_BATCH = 1
DEC_SEQ = 64
PAST_LEN = 512

CHUNK = 64
D_LRU = 512
N_LRU_HEADS = 8
LRU_HEAD_DIM = D_LRU // N_LRU_HEADS
CONV_WIDTH = 4
LRU_C = 8.0
D_S5 = 512
S5_GROUP = 16
N_S5_GROUPS = D_S5 // S5_GROUP
S5_STATE = 64
D_MIX = D_LRU + D_S5
D_IN = 2 * D_LRU + D_S5
PEER_HEADS = 8
PEER_NKEYS = 128
PEER_EXPERTS = PEER_NKEYS * PEER_NKEYS
PEER_DQ = 256
PEER_TOPK = 16
PEER_BLOCK = 256
EPS = 1e-6

kernel_name = "hybrid_rglru_s5_peer_stream_step"

def rmsnorm(x, g):
    xf = x.astype(jnp.float32)
    y = xf * lax.rsqrt(jnp.mean(xf * xf, axis=-1, keepdims=True) + EPS)
    return (y * g.astype(jnp.float32)).astype(x.dtype)

def causal_conv(xa, buf, w, b):
    t = xa.shape[1]
    xp = jnp.concatenate([buf.astype(xa.dtype), xa], axis=1)
    y = b + sum(xp[:, k:k + t] * w[k] for k in range(CONV_WIDTH))
    return y, xp[:, xp.shape[1] - (CONV_WIDTH - 1):]

def _lin_combine(left, right):
    a_l, b_l = left
    a_r, b_r = right
    return a_l * a_r, a_r * b_l + b_r

def _cplx_combine(left, right):
    alr, ali, blr, bli = left
    arr, ari, brr, bri = right
    return (arr * alr - ari * ali, arr * ali + ari * alr,
            arr * blr - ari * bli + brr, arr * bli + ari * blr + bri)

def rglru(xc, h0, w_a, b_a, w_x, b_x, lam):
    f32 = jnp.float32
    bsz, t, _ = xc.shape
    xf = xc.astype(f32)
    xh = xf.reshape(bsz, t, N_LRU_HEADS, LRU_HEAD_DIM)
    r = jax.nn.sigmoid(jnp.einsum("bthi,hij->bthj", xh, w_a.astype(f32)).reshape(bsz, t, D_LRU) + b_a.astype(f32))
    i = jax.nn.sigmoid(jnp.einsum("bthi,hij->bthj", xh, w_x.astype(f32)).reshape(bsz, t, D_LRU) + b_x.astype(f32))
    log_a = -LRU_C * r * jax.nn.softplus(-lam.astype(f32))
    a = jnp.exp(log_a)
    bt = jnp.sqrt(-jnp.expm1(2.0 * log_a)) * (i * xf)
    bt = bt.at[:, 0].add(a[:, 0] * h0.astype(f32))
    _, h = lax.associative_scan(_lin_combine, (a, bt), axis=1)
    return h, h[:, -1]

def s5_scan(u, s0_re, s0_im, a_re, a_im, log_dt, b_re, b_im, c_re, c_im, d):
    f32 = jnp.float32
    bsz, t, _ = u.shape
    ug = u.astype(f32).reshape(bsz, t, N_S5_GROUPS, S5_GROUP)
    lr, li = a_re.astype(f32), a_im.astype(f32)
    dt = jnp.exp(log_dt.astype(f32))[:, None]
    mag = jnp.exp(lr * dt)
    ab_re, ab_im = mag * jnp.cos(li * dt), mag * jnp.sin(li * dt)
    den = lr * lr + li * li
    nr = ab_re - 1.0
    f_re = (nr * lr + ab_im * li) / den
    f_im = (ab_im * lr - nr * li) / den
    br, bi = b_re.astype(f32), b_im.astype(f32)
    bb_re = f_re[..., None] * br - f_im[..., None] * bi
    bb_im = f_re[..., None] * bi + f_im[..., None] * br
    bu_re = jnp.einsum("btgi,gpi->btgp", ug, bb_re)
    bu_im = jnp.einsum("btgi,gpi->btgp", ug, bb_im)
    s0r, s0i = s0_re.astype(f32), s0_im.astype(f32)
    bu_re = bu_re.at[:, 0].add(ab_re * s0r - ab_im * s0i)
    bu_im = bu_im.at[:, 0].add(ab_re * s0i + ab_im * s0r)
    a_re_t = jnp.broadcast_to(ab_re, bu_re.shape)
    a_im_t = jnp.broadcast_to(ab_im, bu_re.shape)
    _, _, s_re, s_im = lax.associative_scan(_cplx_combine, (a_re_t, a_im_t, bu_re, bu_im), axis=1)
    y = (jnp.einsum("btgp,gip->btgi", s_re, c_re.astype(f32))
         - jnp.einsum("btgp,gip->btgi", s_im, c_im.astype(f32))
         + d.astype(f32).reshape(N_S5_GROUPS, S5_GROUP) * ug)
    return y.reshape(bsz, t, D_S5), s_re[:, -1], s_im[:, -1]

def peer(h, w_q, sub_keys, u_tab, v_tab):
    bsz, t, dm = h.shape
    n = bsz * t
    n_pad = -(-n // PEER_BLOCK) * PEER_BLOCK
    hf = jnp.pad(h.reshape(n, dm), ((0, n_pad - n), (0, 0)))
    blocks = hf.reshape(n_pad // PEER_BLOCK, PEER_BLOCK, dm)

    def one_block(xb):
        q = (xb @ w_q).reshape(PEER_BLOCK, PEER_HEADS, 2, PEER_DQ // 2)
        s = jnp.einsum("nhcd,hckd->nhck", q, sub_keys).astype(jnp.float32)
        v1, i1 = lax.top_k(s[:, :, 0], PEER_TOPK)
        v2, i2 = lax.top_k(s[:, :, 1], PEER_TOPK)
        cand = (v1[..., :, None] + v2[..., None, :]).reshape(PEER_BLOCK, PEER_HEADS, PEER_TOPK * PEER_TOPK)
        cidx = (i1[..., :, None] * PEER_NKEYS + i2[..., None, :]).reshape(PEER_BLOCK, PEER_HEADS, PEER_TOPK * PEER_TOPK)
        top_s, pos = lax.top_k(cand, PEER_TOPK)
        eidx = jnp.take_along_axis(cidx, pos, axis=-1)
        gate = jax.nn.softmax(top_s, axis=-1)
        act = jax.nn.gelu(jnp.einsum("nd,nhkd->nhk", xb, u_tab[eidx]).astype(jnp.float32))
        coef = (gate * act).astype(xb.dtype)
        return jnp.einsum("nhk,nhkd->nd", coef, v_tab[eidx])

    out = lax.map(one_block, blocks).reshape(n_pad, dm)[:n]
    return out.reshape(bsz, t, dm).astype(h.dtype)

def trunk_layer(x, c, conv_buf, h0, s0_re, s0_im,
                w_ada, b_ada, norm1, norm2, w_in, conv_w, conv_b,
                lru_wa, lru_ba, lru_wx, lru_bx, lru_lam,
                s5_a_re, s5_a_im, s5_log_dt, s5_b_re, s5_b_im, s5_c_re, s5_c_im, s5_d,
                s5_w_glu, s5_b_glu, gn_lru, gn_s5, w_out,
                peer_wq, peer_keys, peer_u, peer_v):
    mod = (jax.nn.silu(c) @ w_ada + b_ada)[:, None, :]
    sh1, sc1, g1, sh2, sc2, g2 = jnp.split(mod, 6, axis=-1)
    h = rmsnorm(x, norm1) * (1.0 + sc1) + sh1
    z = h @ w_in
    xa = z[..., :D_LRU]
    ga = z[..., D_LRU:2 * D_LRU]
    us = z[..., 2 * D_LRU:]
    xc, new_conv = causal_conv(xa, conv_buf, conv_w, conv_b)
    hl, h_last = rglru(xc, h0, lru_wa, lru_ba, lru_wx, lru_bx, lru_lam)
    y_lru = (hl * jax.nn.gelu(ga.astype(jnp.float32))).astype(x.dtype)
    ys, s_re, s_im = s5_scan(us, s0_re, s0_im, s5_a_re, s5_a_im, s5_log_dt,
                             s5_b_re, s5_b_im, s5_c_re, s5_c_im, s5_d)
    gy = jax.nn.gelu(ys).astype(x.dtype)
    y_s5 = gy * jax.nn.sigmoid(gy @ s5_w_glu + s5_b_glu)
    mix = jnp.concatenate([rmsnorm(y_lru, gn_lru), rmsnorm(y_s5, gn_s5)], axis=-1) @ w_out
    x = x + g1 * mix
    h = rmsnorm(x, norm2) * (1.0 + sc2) + sh2
    x = x + g2 * peer(h, peer_wq, peer_keys, peer_u, peer_v)
    return x, new_conv, h_last, s_re, s_im

def setup_inputs(seed: int = 0) -> dict:
    key = jax.random.key(seed)
    ks = iter(jax.random.split(key, 48))
    f32 = jnp.float32
    d, L, G, P = D_MODEL, DEPTH, N_S5_GROUPS, S5_STATE

    def nrm(shape, scale):
        return jax.random.normal(next(ks), shape, f32) * scale

    x_prompt = nrm((BATCH, SEQ, d), 1.0)
    x_sample = nrm((DEC_BATCH, DEC_SEQ, d), 1.0)
    cache_conv = nrm((L, DEC_BATCH, CONV_WIDTH - 1, D_LRU), 1.0)
    state_lru = nrm((L, DEC_BATCH, D_LRU), 0.5)
    state_s5_re = nrm((L, DEC_BATCH, G, P), 0.1)
    state_s5_im = nrm((L, DEC_BATCH, G, P), 0.1)
    c_prompt = nrm((BATCH, d), 1.0)
    c_sample = nrm((DEC_BATCH, d), 1.0)
    w_ada = nrm((L, d, 6 * d), 0.5 * d ** -0.5)
    b_ada = nrm((L, 6 * d), 0.02)
    norm1 = 1.0 + nrm((L, d), 0.02)
    norm2 = 1.0 + nrm((L, d), 0.02)
    w_in = nrm((L, d, D_IN), d ** -0.5)
    conv_w = nrm((L, CONV_WIDTH, D_LRU), CONV_WIDTH ** -0.5)
    conv_b = nrm((L, D_LRU), 0.02)
    lru_wa = nrm((L, N_LRU_HEADS, LRU_HEAD_DIM, LRU_HEAD_DIM), LRU_HEAD_DIM ** -0.5)
    lru_ba = nrm((L, D_LRU), 0.02)
    lru_wx = nrm((L, N_LRU_HEADS, LRU_HEAD_DIM, LRU_HEAD_DIM), LRU_HEAD_DIM ** -0.5)
    lru_bx = nrm((L, D_LRU), 0.02)
    a_c = jax.random.uniform(next(ks), (L, D_LRU), f32, 0.9, 0.999)
    s_lam = a_c ** (1.0 / LRU_C)
    lru_lam = jnp.log(s_lam) - jnp.log1p(-s_lam)
    s5_a_re = -0.5 + nrm((L, G, P), 0.01)
    s5_a_im = jnp.pi * jnp.arange(P, dtype=f32) + nrm((L, G, P), 0.01)
    s5_log_dt = jax.random.uniform(next(ks), (L, G), f32, math.log(1e-3), math.log(1e-1))
    s5_b_re = nrm((L, G, P, S5_GROUP), (2 * S5_GROUP) ** -0.5)
    s5_b_im = nrm((L, G, P, S5_GROUP), (2 * S5_GROUP) ** -0.5)
    s5_c_re = nrm((L, G, S5_GROUP, P), P ** -0.5)
    s5_c_im = nrm((L, G, S5_GROUP, P), P ** -0.5)
    s5_d = nrm((L, D_S5), 1.0)
    s5_w_glu = nrm((L, D_S5, D_S5), D_S5 ** -0.5)
    s5_b_glu = nrm((L, D_S5), 0.02)
    gn_lru = 1.0 + nrm((L, D_LRU), 0.02)
    gn_s5 = 1.0 + nrm((L, D_S5), 0.02)
    w_out = nrm((L, D_MIX, d), D_MIX ** -0.5)
    peer_wq = nrm((L, d, PEER_HEADS * PEER_DQ), d ** -0.5)
    peer_keys = nrm((L, PEER_HEADS, 2, PEER_NKEYS, PEER_DQ // 2), (PEER_DQ // 2) ** -0.5)
    peer_u = nrm((L, PEER_EXPERTS, d), d ** -0.5)
    peer_v = nrm((L, PEER_EXPERTS, d), PEER_HEADS ** -0.5)
    norm_f = 1.0 + nrm((d,), 0.02)
    return {"x_prompt": x_prompt, "x_sample": x_sample,
            "cache_conv": cache_conv, "state_lru": state_lru,
            "state_s5_re": state_s5_re, "state_s5_im": state_s5_im,
            "c_prompt": c_prompt, "c_sample": c_sample,
            "w_ada": w_ada, "b_ada": b_ada, "norm1": norm1, "norm2": norm2,
            "w_in": w_in, "conv_w": conv_w, "conv_b": conv_b,
            "lru_wa": lru_wa, "lru_ba": lru_ba, "lru_wx": lru_wx, "lru_bx": lru_bx, "lru_lam": lru_lam,
            "s5_a_re": s5_a_re, "s5_a_im": s5_a_im, "s5_log_dt": s5_log_dt,
            "s5_b_re": s5_b_re, "s5_b_im": s5_b_im, "s5_c_re": s5_c_re, "s5_c_im": s5_c_im,
            "s5_d": s5_d, "s5_w_glu": s5_w_glu, "s5_b_glu": s5_b_glu,
            "gn_lru": gn_lru, "gn_s5": gn_s5, "w_out": w_out,
            "peer_wq": peer_wq, "peer_keys": peer_keys, "peer_u": peer_u, "peer_v": peer_v,
            "norm_f": norm_f}

def reference(x_prompt, x_sample, cache_conv, state_lru, state_s5_re, state_s5_im,
              c_prompt, c_sample,
              w_ada, b_ada, norm1, norm2, w_in, conv_w, conv_b,
              lru_wa, lru_ba, lru_wx, lru_bx, lru_lam,
              s5_a_re, s5_a_im, s5_log_dt, s5_b_re, s5_b_im, s5_c_re, s5_c_im, s5_d,
              s5_w_glu, s5_b_glu, gn_lru, gn_s5, w_out,
              peer_wq, peer_keys, peer_u, peer_v, norm_f):
    layer_params = (w_ada, b_ada, norm1, norm2, w_in, conv_w, conv_b,
                    lru_wa, lru_ba, lru_wx, lru_bx, lru_lam,
                    s5_a_re, s5_a_im, s5_log_dt, s5_b_re, s5_b_im, s5_c_re, s5_c_im, s5_d,
                    s5_w_glu, s5_b_glu, gn_lru, gn_s5, w_out,
                    peer_wq, peer_keys, peer_u, peer_v)

    def run(x, c, conv, hl, sr, si):
        convs, hs, srs, sis = [], [], [], []
        for l in range(DEPTH):
            x, nc, nh, nsr, nsi = trunk_layer(x, c, conv[l], hl[l], sr[l], si[l],
                                              *[p[l] for p in layer_params])
            convs.append(nc)
            hs.append(nh)
            srs.append(nsr)
            sis.append(nsi)
        return (rmsnorm(x, norm_f), jnp.stack(convs), jnp.stack(hs),
                jnp.stack(srs), jnp.stack(sis))

    bp = x_prompt.shape[0]
    zero_conv = jnp.zeros((DEPTH, bp, CONV_WIDTH - 1, D_LRU), x_prompt.dtype)
    zero_lru = jnp.zeros((DEPTH, bp, D_LRU), jnp.float32)
    zero_s5 = jnp.zeros((DEPTH, bp, N_S5_GROUPS, S5_STATE), jnp.float32)
    y_prompt, conv_p, lru_p, s5re_p, s5im_p = run(x_prompt, c_prompt, zero_conv, zero_lru, zero_s5, zero_s5)
    y_sample, conv_s, lru_s, s5re_s, s5im_s = run(x_sample, c_sample, cache_conv, state_lru,
                                                  state_s5_re, state_s5_im)
    return (y_prompt, y_sample, conv_p, lru_p, s5re_p, s5im_p, conv_s, lru_s, s5re_s, s5im_s)


_drawn_inputs = setup_inputs


def setup_inputs(seed=0):
    import zlib

    import numpy as np

    out = dict(_drawn_inputs(seed))
    spreads = {}
    factors = {'norm1': 2.956,
     'norm2': 7.076,
     'lru_ba': 8.0,
     'lru_bx': 8.0,
     's5_a_re': 4.589,
     's5_c_re': 3.082,
     's5_c_im': 3.017,
     's5_b_glu': 8.0,
     'gn_lru': 8.0,
     'gn_s5': 8.0,
     'norm_f': 2.713}
    for name, (base, spread) in spreads.items():
        noise = np.random.default_rng([zlib.crc32(name.encode()), seed]).standard_normal(out[name].shape)
        drawn = base * np.exp(spread * noise) if base else spread * noise
        out[name] = __import__('jax').numpy.asarray(drawn.astype(out[name].dtype))
    for name, factor in factors.items():
        out[name] = (out[name] * factor).astype(out[name].dtype)
    return out
```

```python
from contextlib import ExitStack

import concourse.bass as bass
from concourse import mybir

F32 = mybir.dt.float32
U32 = mybir.dt.uint32
ALU = mybir.AluOpType
ACT = mybir.ActivationFunctionType
AX = mybir.AxisListType

P = 128
DM = 1024
DK = DM // P
SEQ, DSEQ = 1024, 64
NT = SEQ + DSEQ
L = 8
NC, NCS = SEQ // L, DSEQ // L
DL = 512
ML = DL // P
DIN = 3 * DL
CW = 4
LRU_C = 8.0
G, GS, SP = 32, 16, 64
PAIRS = G // 2
HEADS, TOPK, NKEYS = 8, 16, 128
NTILE = 9
EPS = 1e-6
SLOTS = NC + 1 + NCS + 1
SFLAT = PAIRS * SLOTS
CHUNKS = [(0, 3, 384), (3, 3, 384), (6, 2, 320)]
TWO_PI = 6.283185307179586
MAGIC = 12582912.0
NEG = -3.0e38
NLINK = 41

PACK = {}
_at = 0
for _n, _w in (("cT", 16), ("norm1", 8), ("norm2", 8), ("conv_w", 16), ("conv_b", 4), ("ba", 4), ("bx", 4),
               ("lam", 4), ("bglu", 4), ("gnl", 4), ("gns", 4), ("h0", 4), ("cache", 12), ("are", 16), ("aim", 16),
               ("ldt", 16), ("s0re", 16), ("s0im", 16), ("bre", 256), ("bim", 256), ("cre", 256), ("cim", 256),
               ("wa", 512), ("wx", 512)):
    PACK[_n] = (_at, _at + _w)
    _at += _w
NPACK = _at

ARENA = 48900
X0 = 0
XN = 9216
WADA = 9216
WIN = 18432
MROW, BROW = 30720, 36864
HT = 30720
XAP, XAS, GA = 9216, 13324, 13592
UT_, US_, U8_ = 0, 4096, 4608
XC, RG, IG, TG, HS = 18432, 22784, 27136, 31488, 35840
YL = 40192
OC, XR, TMP, RT, UG, TT, K0 = 9216, 13824, 18240, 22848, 26944, 31296, 35392
VV, MD, EE = XR, K0, 0
YT_, YS_, Y8_ = 0, 4096, 4608
GYT, YS5, WGLU, WOUT, X1, MT, SQ = 9216, 13568, 17920, 19968, 28160, 37376, 0
XN2, H2T = 9216, 0
G1B = 46852
WQ, KEYS, QT, SB, WK, CAND, CW2, D1, D2, D3, IALL = (8704, 12800, 14848, 17024, 19328, 20480, 22784, 25088, 27392,
                                                     29696, 32000)
ITR = 35456
PB, QB, CB = 8704, 10752, 12800
UB, VB, CBD, WB, YB = 8704, 12800, 16896, 21248, 25600
XL, NF = 0, 40192
JUNK, DDG, SEL = 45000, 46024, 46536


def trunk(nc, A, O):
    with ExitStack() as ctx:
        def sb(name, shape, dt=F32):
            return ctx.enter_context(nc.sbuf_tensor(name, shape, dt))

        def sem(name):
            return ctx.enter_context(nc.semaphore(name))

        arena = sb("arena", [P, ARENA])
        prm = sb("prm", [P, NPACK])
        ident = sb("ident", [P, P])
        ones = sb("ones", [P, 1])
        iota = sb("iota", [P, P])
        mcol = sb("mcol", [P, 48, 2])
        csil = sb("csil", [P, 16])
        a1 = sb("a1", [P, DK, 2])
        a2 = sb("a2", [P, DK, 2])
        s5c = sb("s5c", [P, 24, PAIRS])
        bb = sb("bb", [P, 2, 256])
        pw = sb("pw", [P, 2, PAIRS, 9])
        pwr = sb("pwr", [P, 2, PAIRS, 8])
        ssq = sb("ssq", [P, 4 * NTILE])
        lrc = sb("lrc", [P, 24])
        fin = sb("fin", [P, 72])
        rms3 = sb("rms3", [P, 30])
        rms4 = sb("rms4", [P, 30])
        ps = [ctx.enter_context(nc.psum_tensor(f"ps{i}", [P, 512], F32)) for i in range(8)]

        coef = nc.dram_tensor("coef_dram", (64, P, 17, 2, 64), F32, kind="Internal").ap()
        x1d = nc.dram_tensor("x1_dram", (P, 9216), F32, kind="Internal").ap()

        def ar(off, n, parts=P):
            return arena[0:parts, off:off + n]

        def par(name, parts=P):
            return prm[0:parts, PACK[name][0]:PACK[name][1]]

        ddg = ar(DDG, DL, GS)
        sel = ar(SEL, 2 * P, 2).rearrange("p (r n) -> p r n", r=2)
        junk, tmp256 = ar(JUNK, 1024), ar(JUNK - 256, 256)
        small = {}
        at = ITR + 3 * NT
        for name, w in (("vtop", 288), ("itop", 288), ("itf", 288), ("mark", 8), ("smx", 144), ("mx1", NTILE),
                        ("pos", 144), ("posab", 288), ("pf", 288), ("pick", 144)):
            small[name] = ar(at, w)
            at += w
        assert at <= G1B
        two = lambda v: v.rearrange("p (c t k) -> p c t k", c=2, t=NTILE)
        one = lambda v: v.rearrange("p (t k) -> p t k", t=NTILE)
        vtop, itf, pf, mark = two(small["vtop"]), two(small["itf"]), two(small["pf"]), small["mark"]
        itop, posab = two(small["itop"].bitcast(U32)), two(small["posab"].bitcast(U32))
        smx, mx1, pick, pos = one(small["smx"]), one(small["mx1"]), one(small["pick"]), one(small["pos"].bitcast(U32))

        S = {}

        def s(name):
            if name not in S:
                S[name] = sem(name)
            return S[name]

        plan, where = [], {}

        def jobs(stage, n, who):
            for i in range(n):
                where[stage, i] = len(plan)
                plan.append(who(i) if callable(who) else who)

        jobs("mod", 12, "dve")
        jobs("modT", 1, "act")
        jobs("g1", 4, "act")
        jobs("h1T", 24, lambda i: "act" if i % 2 else "dve")
        jobs("z", 24, lambda i: "dve" if i < 12 else "act")
        jobs("us", 9, "act")
        jobs("gate", 24, "act")
        jobs("k0", 8, "act")
        jobs("rt", 8, "act")
        jobs("ug", 11, "act")
        jobs("v", 16, "dve")
        jobs("y", 16, "act")
        jobs("gyT", 12, "dve")
        jobs("glu", 12, "act")
        jobs("rms", 1, "dve")
        jobs("mix", 36, "dve")
        jobs("h2T", 24, lambda i: "act" if i % 2 else "dve")
        n_stage = {}
        for (stage, i) in where:
            n_stage[stage] = max(n_stage.get(stage, 0), i + 1)
        emptied = {"act": s("banks_emptied_by_act"), "dve": s("banks_emptied_by_dve")}
        bank_full = s("bank_full")

        def empties(upto, e):
            return sum(p == e for p in plan[:upto])

        def bank_for(pe, stage, i):
            j = where[stage, i]
            if j >= 8:
                pe.wait_ge(emptied[plan[j - 8]], empties(j - 7, plan[j - 8]))
            return ps[j % 8]

        def filled(eng, stage, i):
            j = where[stage, i]
            eng.wait_ge(bank_full, j + 1)
            return ps[j % 8]

        def stage_emptied(eng, stage, n=None):
            upto = where[stage, (n or n_stage[stage]) - 1] + 1
            for e in ("act", "dve"):
                if empties(upto, e):
                    eng.wait_ge(emptied[e], empties(upto, e))

        block = ctx.enter_context(nc.Block())

        def group(q, e):
            return 8 * (q // 2) + 2 * e + q % 2

        def cols(t):
            return (t * P, P) if t < 8 else (SEQ, DSEQ)

        def modulated(eng, who, stage, dst, sc, sh):
            for j in range(8):
                for q in range(3):
                    if plan[where[stage, 3 * j + q]] != who:
                        continue
                    b = filled(eng, stage, 3 * j + q)
                    width, g = (512, 0) if q < 2 else (DSEQ, 1)
                    out = ar(dst + NT * j + 512 * q, width)
                    if who == "act":
                        nc.scalar.activation(out, b[:, 0:width], ACT.Identity, bias=mcol[:, sh + j, g:g + 1],
                                scale=sc[:, j, g:g + 1]).then_inc(emptied["act"], 1)
                    else:
                        nc.vector.tensor_scalar(out, b[:, 0:width], sc[:, j, g:g + 1], mcol[:, sh + j, g:g + 1],
                                                ALU.mult, ALU.add).then_inc(emptied["dve"], 1)

        @block.sync
        def _(sp):
            def load(dst, src, name, n=16):
                sp.dma_start(dst, src).then_inc(s(name), n)

            load(prm[:, :], A["pack"], "params_in")
            load(ar(BROW, 6144, 2), A["b_ada"], "b_ada_in")
            load(ddg, A["ddiag"], "params_in")
            wv = A["w_ada"].rearrange("(k p) n -> p k n", p=P)
            for n in range(12):
                if n >= 2:
                    sp.wait_ge(bank_full, where["mod", n - 2] + 1)
                load(ar(WADA + 4096 * (n % 2), 4096).rearrange("p (k n) -> p k n", k=8),
                     wv[:, :, 512 * n:512 * n + 512], f"w_ada_in{n % 2}")
                if n == 3:
                    load(ar(X0, 8192).rearrange("p (k d) -> p k d", k=8), A["xp"], "x_in")
                    load(ar(X0 + 8192, 1024, DSEQ), A["xs"], "x_in")
                if n == 5:
                    load(ar(WIN, 12288).rearrange("p (k n) -> p k n", k=8),
                         A["w_in"].rearrange("(k p) n -> p k n", p=P), "w_in_in")
            stage_emptied(sp, "us")
            for k in range(L):
                load(ar(U8_, 4096, NCS).rearrange("p (g k i) -> p k g i", g=G, k=L)[:, k],
                     arena[8 * k:8 * k + 8, US_:US_ + 512].rearrange("p (g i) -> p g i", g=G), "u8_in")
            with nc.allow_non_contiguous_dma(reason="last rows of a channel-major buffer"):
                stage_emptied(sp, "z", 12)
                for m in range(ML):
                    sp.dma_start(O["conv_p"][:, m, :], ar(XAP + 1027 * m + 1024, 3)).then_inc(s("states_out"), 16)
                    sp.dma_start(O["conv_s"][:, m, :], ar(XAS + 67 * m + 64, 3)).then_inc(s("states_out"), 16)
            sp.wait_ge(s("k0_ready"), 1)
            sp.wait_ge(s("t_zeroed"), 1)
            tv = ar(TT, 4096).rearrange("p (g n) -> p g n", g=G)
            kv = ar(K0, 4096, GS).rearrange("p (g n) -> p g n", g=G)
            for j in range(L):
                load(tv[GS * j:GS * j + GS, :, GS * j:P], kv[:, :, 0:P - GS * j], "toeplitz_in")
            stage_emptied(sp, "y")
            for k in range(L):
                load(arena[8 * k:8 * k + 8, YS_:YS_ + 512], ar(Y8_ + 512 * k, 512, NCS), "ys_in")
            sp.wait_ge(s("fin_ready"), 2)
            sp.dma_start(O["fin"], fin[:, :]).then_inc(s("states_out"), 16)
            load(ar(WGLU, 2048).rearrange("p (k n) -> p k n", k=4), A["w_glu"].rearrange("(k p) n -> p k n", p=P),
                 "w_glu_in")
            load(ar(WOUT, 8192).rearrange("p (k n) -> p k n", k=8), A["w_out"].rearrange("(k p) n -> p k n", p=P),
                 "w_out_in")
            load(ar(X1, 8192).rearrange("p (k d) -> p k d", k=8), A["xp"], "x_again_in")
            load(ar(X1 + 8192, 1024, DSEQ), A["xs"], "x_again_in")
            sp.wait_ge(s("x1_ready"), NTILE)
            sp.dma_start(x1d[:, 0:8192], ar(X1, 8192)).then_inc(s("x1_out"), 16)
            sp.dma_start(x1d[0:DSEQ, 8192:9216], ar(X1 + 8192, 1024, DSEQ)).then_inc(s("x1_out"), 16)
            sp.wait_ge(s("x1_out"), 32)
            stage_emptied(sp, "h2T")
            load(ar(KEYS, 2048), A["keys"], "keys_in")
            for h in range(2):
                load(ar(WQ + 2048 * h, 2048), A["wq"][h], f"wq_in{h}")
            with sp.Fori(0, HEADS // 2 - 1) as i:
                for h in range(2):
                    sp.wait_ge(s("s_full"), 4 * i + 2 * h + 2)
                    load(ar(WQ + 2048 * h, 2048), A["wq"][bass.ds(2 * i + (2 + h), 1)].rearrange("h p n -> (h p) n"),
                         f"wq_in{h}")

            def store_block(b, buf):
                sp.wait_ge(s("c_moved"), 16 * b + 16)
                sp.dma_start(coef[:, :, bass.ds(b, 1), :, :].rearrange("g p b e n -> p g (b e n)"),
                             ar(CB + 8192 * buf, 8192).rearrange("p (g n) -> p g n", g=64)).then_inc(
                    s(f"coef_out{buf}"), 16)

            with sp.Fori(0, 8) as i:
                store_block(2 * i, 0)
                store_block(2 * i + 1, 1)
            store_block(16, 0)
            sp.wait_ge(s("coef_out0"), 16 * 9)
            sp.wait_ge(s("coef_out1"), 16 * 8)

            def load_experts(t, u, i, first):
                if not first:
                    sp.wait_ge(s("s_bank_full"), 6 * (t - 1))
                load(ar(UB + 2048 * u, 2048), A["ut"][bass.ds(t, 1)].rearrange("t p n -> (t p) n"), f"u_in{u}")
                if not first:
                    sp.wait_ge(s("w_ready"), 6 * (t - 1))
                load(ar(CBD + 2176 * u, 2176), coef[bass.ds(t, 1)].rearrange("t p b e n -> (t p) (b e n)"), f"c_in{u}")
                if not first:
                    sp.wait_ge(s("v_bank_full"), 24 * (t - 1))
                load(ar(VB + 2048 * u, 2048), A["vt"][bass.ds(t, 1)].rearrange("t p n -> (t p) n"), f"v_in{u}")

            load_experts(0, 0, 0, True)
            load_experts(1, 1, 0, True)
            with sp.Fori(1, 32) as i:
                load_experts(2 * i, 0, i, False)
                load_experts(2 * i + 1, 1, i, False)
            sp.wait_ge(s("v_bank_full"), 24 * 64)
            load(ar(XL, 8192), x1d[:, 0:8192], "x1_back")
            load(ar(XL + 8192, 1024, DSEQ), x1d[0:DSEQ, 8192:9216], "x1_back")
            load(ar(NF, 1024), A["norm_f"], "norm_f_in")
            for t in range(8):
                sp.wait_ge(s("y_ready"), t + 1)
                sp.dma_start(O["yp"][:, t, :], ar(XL + 1024 * t, 1024)).then_inc(s("y_out"), 16)
            sp.wait_ge(s("y_ready"), 9)
            sp.dma_start(O["ys"], ar(XL + 8192, 1024, DSEQ)).then_inc(s("y_out"), 16)
            sp.wait_ge(s("y_out"), 16 * 9)
            sp.wait_ge(s("states_out"), 16 * 9)

        @block.gpsimd
        def _(pool):
            nc.gpsimd.memset(ident[:, :], 0.0).then_inc(s("ident_zero"), 1)
            nc.gpsimd.memset(ones[:, :], 1.0).then_inc(s("const_ready"), 1)
            nc.gpsimd.iota(iota[:, :], [[1, P]], base=0, channel_multiplier=0,
                           allow_small_or_imprecise_dtypes=True).then_inc(s("const_ready"), 1)
            pool.wait_ge(s("ident_zero"), 1)
            nc.gpsimd.affine_select(out=ident[:, :], in_=ident[:, :], compare_op=ALU.not_equal, fill=1.0, base=0,
                                    pattern=[[-1, P]], channel_multiplier=1).then_inc(s("const_ready"), 1)
            pool.wait_ge(s("const_ready"), 3)
            for r in range(2):
                nc.gpsimd.tensor_copy(sel[:, r, :], ident[0:2, r:r + 1].to_broadcast([2, P])).then_inc(
                    s("const_ready"), 1)

        @block.tensor
        def _(pe):
            mm = nc.tensor.matmul
            full = lambda ins: ins.then_inc(bank_full, 1)
            pe.wait_ge(s("csil_ready"), 1)
            cs = csil[:, :].rearrange("p (k s) -> p k s", s=2)
            for n in range(12):
                pe.wait_ge(s(f"w_ada_in{n % 2}"), 16 * (n // 2 + 1))
                b = bank_for(pe, "mod", n)
                w = ar(WADA + 4096 * (n % 2), 4096).rearrange("p (k n) -> p k n", k=8)
                for k in range(8):
                    last = mm(b[0:2, :], cs[:, k, :], w[:, k, :], start=k == 0, stop=k == 7)
                full(last)
            pe.wait_ge(s("const_ready"), 5)
            stage_emptied(pe, "mod")
            b = bank_for(pe, "modT", 0)
            for j in range(48):
                last = mm(b[:, 2 * j:2 * j + 2], ar(MROW + P * j, P, 2), ident[0:2, 0:2], start=True, stop=True)
            full(last)
            for q in range(4):
                b = bank_for(pe, "g1", q)
                full(mm(b[:, :], sel[:, q // 2, :],
                        ar(MROW + 2048 + 512 * (q % 2), 512, 2), start=True, stop=True))

            def turn(stage, nd, src, srcs):
                for j in range(nd):
                    for q in range(3):
                        b = bank_for(pe, stage, 3 * j + q)
                        if q < 2:
                            for t in range(4):
                                last = nc.tensor.transpose(b[:, P * t:P * t + P], src(4 * q + t, j), ident[:, :])
                        else:
                            last = nc.tensor.transpose(b[:, 0:DSEQ], srcs(j), ident[0:DSEQ, 0:DSEQ])
                        full(last)

            pe.wait_ge(s("xn_ready"), NTILE)
            turn("h1T", 8, lambda t, j: ar(XN + 1024 * t + P * j, P), lambda j: ar(XN + 8192 + P * j, P, DSEQ))
            stage_emptied(pe, "h1T")
            pe.wait_ge(s("w_in_in"), 16)
            w = ar(WIN, 12288).rearrange("p (k n) -> p k n", k=8)
            h = ar(HT, 8704).rearrange("p (k n) -> p k n", k=8)
            for m in range(8):
                for q, (k0, nk, width) in enumerate(CHUNKS):
                    b = bank_for(pe, "z", 3 * m + q)
                    for k in range(8):
                        last = mm(b[:, 0:width], w[:, k, P * m:P * m + P], h[:, k, P * k0:P * k0 + width],
                                  start=k == 0, stop=k == 7)
                    full(last)
            for t in range(NTILE):
                b = bank_for(pe, "us", t)
                c0, n = cols(t)
                for k in range(8):
                    last = mm(b[0:n, :], h[:, k, c0:c0 + n], w[:, k, 1024:1536], start=k == 0, stop=k == 7)
                full(last)
            for m in range(ML):
                pe.wait_ge(s("xc_ready"), 2 * (m + 1))
                for gate, name in enumerate(("wa", "wx")):
                    for q in range(3):
                        b = bank_for(pe, "gate", 6 * m + 3 * gate + q)
                        width = CHUNKS[q][2]
                        full(mm(b[:, 0:width], par(name)[:, P * m:P * m + P],
                                ar(XC + NT * m + 384 * q, width), start=True, stop=True))
            pe.wait_ge(s("oc_ready"), 1)
            oc = [ar(OC + 2304 * r, 2304).rearrange("p (a n) -> p a n", a=PAIRS) for r in range(2)]
            for q in range(8):
                b = bank_for(pe, "k0", q)
                for e in range(4):
                    g = group(q, e)
                    lo, pair = 64 * (g % 2), g // 2
                    for r in range(2):
                        last = mm(b[0:GS, P * e:P * e + P],
                                  bb[lo:lo + 64, r, GS * pair:GS * pair + GS], oc[r][lo:lo + 64, pair, 0:P],
                                  start=r == 0, stop=r == 1)
                full(last)
            pe.wait_ge(s("xr_ready"), 1)
            for q in range(8):
                b = bank_for(pe, "rt", q)
                for n in range(4):
                    pair, r = (4 * q + n) // 2, n % 2
                    last = nc.tensor.transpose(b[:, P * n:P * n + P], ar(XR + 2048 * r + P * pair, P), ident[:, :])
                full(last)
            stage_emptied(pe, "us")
            pe.wait_ge(s("u8_in"), 16 * L)
            uv = ar(UT_, 4096).rearrange("p (g n) -> p g n", g=G)
            u8 = ar(U8_, 4096, NCS).rearrange("p (g n) -> p g n", g=G)
            for q in range(11):
                b = bank_for(pe, "ug", q)
                for n, g in enumerate(range(3 * q, min(3 * q + 3, G))):
                    nc.tensor.transpose(b[:, 136 * n:136 * n + P], uv[:, g], ident[:, :])
                    last = nc.tensor.transpose(b[:, 136 * n + P:136 * n + 136], u8[:, g], ident[0:NCS, 0:NCS])
                full(last)
            stage_emptied(pe, "ug")
            rt = ar(RT, 4096).rearrange("p (a r n) -> p a r n", a=PAIRS, r=2)
            ug = ar(UG, 4352).rearrange("p (g n) -> p g n", g=G)
            for a in range(PAIRS):
                b = bank_for(pe, "v", a)
                for e in range(2):
                    for r in range(2):
                        last = mm(b[64 * e:64 * e + 64, 136 * r:136 * r + 136], rt[:, a, r, 64 * e:64 * e + 64],
                                  ug[:, 2 * a + e, :], start=True, stop=True)
                full(last)
            pe.wait_ge(s("toeplitz_in"), 16 * L)
            pe.wait_ge(s("state_ready"), 1)
            tt = ar(TT, 4096).rearrange("p (g n) -> p g n", g=G)
            st = [ar(VV + SFLAT * r, SFLAT).rearrange("p (a n) -> p a n", a=PAIRS) for r in range(2)]
            for q in range(16):
                b = bank_for(pe, "y", q)
                u0, s0, n = ((0, 0, NC), (NC, NC + 1, NCS))[q // 8]
                for e in range(4):
                    g = group(q % 8, e)
                    lo, pair = 64 * (g % 2), g // 2
                    out = b[0:n, P * e:P * e + P]
                    mm(out, ug[:, g, u0:u0 + n], tt[:, g, :], start=True, stop=False)
                    for r in range(2):
                        last = mm(out, st[r][lo:lo + 64, pair, s0:s0 + n], oc[r][lo:lo + 64, pair, GS:GS + P],
                                  start=False, stop=r == 1)
                full(last)
            stage_emptied(pe, "y")
            pe.wait_ge(s("ys_in"), 16 * L)
            turn("gyT", 4, lambda t, j: ar(YT_ + 512 * t + P * j, P), lambda j: ar(YS_ + P * j, P, DSEQ))
            stage_emptied(pe, "gyT")
            pe.wait_ge(s("w_glu_in"), 16)
            w = ar(WGLU, 2048).rearrange("p (k n) -> p k n", k=4)
            for m in range(ML):
                for q, (k0, nk, width) in enumerate(CHUNKS):
                    b = bank_for(pe, "glu", 3 * m + q)
                    for k in range(4):
                        last = mm(b[:, 0:width], w[:, k, P * m:P * m + P], ar(GYT + NT * k + P * k0, width),
                                  start=k == 0, stop=k == 3)
                    full(last)
            b = bank_for(pe, "rms", 0)
            for half in range(2):
                pe.wait_ge(s("sq_ready"), half + 1)
                for t in range(NTILE):
                    c0, n = cols(t)
                    for k in range(4):
                        last = mm(b[0:n, 9 * half + t:9 * half + t + 1], ar(SQ + 4352 * half + NT * k + c0, n),
                                  ones[:, :], start=k == 0, stop=k == 3)
            full(last)
            pe.wait_ge(s("halves_scaled"), 2)
            pe.wait_ge(s("w_out_in"), 16)
            w = ar(WOUT, 8192).rearrange("p (k n) -> p k n", k=8)
            for t in range(NTILE):
                c0, n = cols(t)
                for nh in range(2):
                    for half, src in enumerate((YL, YS5)):
                        b = bank_for(pe, "mix", 4 * t + 2 * nh + half)
                        for k in range(4):
                            last = mm(b[0:n, :], ar(src + NT * k + c0, n), w[:, 4 * half + k, 512 * nh:512 * nh + 512],
                                      start=k == 0, stop=k == 3)
                        full(last)
            pe.wait_ge(s("xn2_ready"), NTILE)
            turn("h2T", 8, lambda t, j: ar(XN2 + 1024 * t + P * j, P), lambda j: ar(XN2 + 8192 + P * j, P, DSEQ))
            stage_emptied(pe, "h2T")

            h2 = ar(H2T, 8704).rearrange("p (k n) -> p k n", k=8)
            pe.wait_ge(s("keys_in"), 16)

            def head(hd, hb, i, first=False):
                pe.wait_ge(s("kbuf_ready"), hd + 1)
                pe.wait_ge(s(f"wq_in{hb}"), 16 * i + 16)
                for c in range(2):
                    w = ar(WQ + 2048 * hb + 1024 * c, 1024).rearrange("p (k n) -> p k n", k=8)
                    for q, (k0, nk, width) in enumerate(CHUNKS):
                        for k in range(8):
                            last = mm(ps[q][:, 0:width], w[:, k, :], h2[:, k, P * k0:P * k0 + width],
                                      start=k == 0, stop=k == 7)
                    last.then_inc(s("q_full"), 1)
                    pe.wait_ge(s("q_moved"), 2 * hd + c + 1)
                    if not (first and c == 0):
                        pe.wait_ge(s("s_moved"), 2 * hd + c)
                    for t in range(NTILE):
                        c0, n = cols(t)
                        last = mm(ps[3 + t // 4][0:n, P * (t % 4):P * (t % 4) + P], ar(QT + NT * c + c0, n),
                                  kbuf[:, c, :], start=True, stop=True)
                    last.then_inc(s("s_full"), 1)

            kbuf = ar(WK, 256).rearrange("p (c n) -> p c n", c=2)

            head(0, 0, 0, True)
            head(1, 1, 0)
            with pe.Fori(1, HEADS // 2) as i:
                head(2 * i, 0, i)
                head(2 * i + 1, 1, i)

            pe.wait_ge(s("picks_ready"), HEADS)
            for a in range(3):
                for q in range(3):
                    if 3 * a + q == 8:
                        pe.wait_ge(s("picksT_moved"), 1)
                    for t in range(4 * q, min(4 * q + 4, NTILE)):
                        c0, n = cols(t)
                        last = nc.tensor.transpose(ps[(3 * a + q) % 8][:, P * (t % 4):P * (t % 4) + n],
                                                   ar(IALL + 1152 * a + P * t, P, n), ident[0:n, 0:n])
                    last.then_inc(s("picksT_full"), 1)

            pe.wait_ge(s("picksT_moved"), 9)

            def coef_block(b, first):
                for g in range(8):
                    pe.wait_ge(s("onehot_ready"), 16 * b + 2 * g + 2)
                    if not (first and g < 4):
                        pe.wait_ge(s("c_moved"), 16 * b + 2 * g - 6)
                    for j in range(8):
                        bank = ps[2 * (g % 4) + j // 4]
                        last = mm(bank[:, P * (j % 4):P * (j % 4) + P], ar(PB + 1024 * (g % 2) + P * j, P),
                                  ar(QB + 1024 * (g % 2) + P * j, P), start=True, stop=True)
                    last.then_inc(s("c_full"), 1)

            coef_block(0, True)
            coef_block(1, False)
            with pe.Fori(1, 8) as i:
                coef_block(2 * i, False)
                coef_block(2 * i + 1, False)
            coef_block(16, False)
            pe.wait_ge(s("c_moved"), 16 * 17)

            def scores(t, u, i, first):
                pe.wait_ge(s(f"u_in{u}"), 16 * i + 16)
                w = ar(UB + 2048 * u, 2048).rearrange("p (e k n) -> p e k n", e=2, k=8)
                for e in range(2):
                    for q, (k0, nk, width) in enumerate(CHUNKS):
                        j = 3 * e + q
                        if not (first and j < 4):
                            pe.wait_ge(s("s_gelu"), 6 * t + j - 3)
                        for k in range(8):
                            last = mm(ps[(6 * u + j) % 4][:, 0:width], w[:, e, k, :], h2[:, k, P * k0:P * k0 + width],
                                      start=k == 0, stop=k == 7)
                        last.then_inc(s("s_bank_full"), 1)

            def values(t, u, i, first):
                pe.wait_ge(s(f"v_in{u}"), 16 * i + 16)
                pe.wait_ge(s("w_ready"), 6 * t + 6)
                w = ar(VB + 2048 * u, 2048).rearrange("p (e n) -> p e n", e=2)
                for d in range(8):
                    for q, (k0, nk, width) in enumerate(CHUNKS):
                        j = 3 * d + q
                        if not (first and j < 4):
                            pe.wait_ge(s("y_added"), 24 * t + j - 3)
                        for e in range(2):
                            last = mm(ps[4 + j % 4][:, 0:width], w[:, e, P * d:P * d + P],
                                      ar(WB + 2176 * u + NT * e + P * k0, width), start=e == 0, stop=e == 1)
                        last.then_inc(s("v_bank_full"), 1)

            scores(0, 0, 0, True)
            scores(1, 1, 0, False)
            values(0, 0, 0, True)
            with pe.Fori(1, 32) as i:
                scores(2 * i, 0, i, False)
                values(2 * i - 1, 1, i - 1, False)
                scores(2 * i + 1, 1, i, False)
                values(2 * i, 0, i, False)
            values(63, 1, 31, False)
            for t in range(NTILE):
                c0, n = cols(t)
                if t == 0:
                    pe.wait_ge(s("y_scaled"), 1)
                if t >= 4:
                    pe.wait_ge(s("x2_done"), t - 3)
                for d in range(8):
                    last = nc.tensor.transpose(ps[2 * (t % 4) + d // 4][0:n, P * (d % 4):P * (d % 4) + P],
                                               ar(YB + NT * d + c0, n), ident[:, :])
                last.then_inc(s("yT_full"), 1)

        @block.scalar
        def _(act):
            av = nc.scalar.activation
            done = lambda ins: ins.then_inc(emptied["act"], 1)
            act.wait_ge(s("params_in"), 32)
            av(csil[:, :], par("cT"), ACT.Sigmoid).then_inc(s("csig_ready"), 1)
            av(s5c[:, 0, :], par("ldt"), ACT.Exp).then_inc(s("s5_dt_ready"), 1)
            act.wait_ge(s("s5_lrdt_ready"), 1)
            av(s5c[:, 3, :], s5c[:, 1, :], ACT.Exp).then_inc(s("s5_mag_ready"), 1)
            av(s5c[:, 4, :], s5c[:, 1, :], ACT.Exp, scale=float(L)).then_inc(s("s5_mag_ready"), 1)
            act.wait_ge(s("lam_abs_ready"), 1)
            av(lrc[:, 4:8], lrc[:, 0:4], ACT.Exp, scale=-1.0).then_inc(s("lam_exp_ready"), 1)
            act.wait_ge(s("lam_w_ready"), 1)
            av(lrc[:, 12:16], lrc[:, 8:12], ACT.Ln).then_inc(s("lam_ln_ready"), 1)
            for f in range(2):
                act.wait_ge(s("phase_ready"), f + 1)
                av(s5c[:, 8 + 4 * f, :], s5c[:, 7 + 4 * f, :], ACT.Sin).then_inc(s("sin_ready"), 1)
                av(s5c[:, 9 + 4 * f, :], s5c[:, 7 + 4 * f, :], ACT.Sin, scale=0.5).then_inc(s("sin_ready"), 1)
            b = filled(act, "modT", 0)
            done(nc.scalar.copy(mcol[:, :, :].rearrange("p j s -> p (j s)"), b[:, 0:96]))
            for q in range(4):
                b = filled(act, "g1", q)
                done(nc.scalar.copy(ar(G1B + 512 * q, 512), b[:, :]))
            act.wait_ge(s("x_in"), 32)
            for t in range(NTILE):
                n = cols(t)[1]
                if t:
                    act.wait_ge(s("ssq1"), t)
                av(junk[0:n, :], ar(X0 + 1024 * t, 1024, n), ACT.Square, accum_out=ssq[0:n, t:t + 1]).then_inc(
                    s("ssq1"), 1)
            act.wait_ge(s("ms1_ready"), 2)
            av(ssq[:, 18:26], ssq[:, 9:17], ACT.Sqrt).then_inc(s("rt1_ready"), 1)
            av(ssq[0:DSEQ, 26:27], ssq[0:DSEQ, 17:18], ACT.Sqrt).then_inc(s("rt1_ready"), 1)

            act.wait_ge(s("a1_ready"), 1)
            stage_emptied(act, "g1")
            modulated(act, "act", "h1T", HT, a1, 0)
            for m in range(4):
                for q, (k0, nk, width) in enumerate(CHUNKS):
                    b = filled(act, "z", 12 + 3 * m + q)
                    out = ar(GA + NT * m, SEQ).rearrange("p (c k) -> p k c", k=L)[:, k0:k0 + nk, :]
                    last = av(out, b[:, 0:P * nk].rearrange("p (k c) -> p k c", k=nk), ACT.Gelu_apprx_tanh)
                    if q == 2:
                        out = ar(GA + NT * m + SEQ, DSEQ).rearrange("p (c k) -> p k c", k=L)
                        last = av(out, b[:, 256:320].rearrange("p (k c) -> p k c", k=L), ACT.Gelu_apprx_tanh)
                    done(last)
            for t in range(NTILE):
                b = filled(act, "us", t)
                n = cols(t)[1]
                if t < 8:
                    done(nc.scalar.copy(ar(UT_, 4096).rearrange("p (g k i) -> p k g i", g=G, k=L)[:, t],
                                        b[:, :].rearrange("p (g i) -> p g i", g=G)))
                else:
                    done(nc.scalar.copy(ar(US_, 512, n), b[0:n, :]))
            for m in range(ML):
                for gate, (dst, bias) in enumerate(((RG, "ba"), (IG, "bx"))):
                    for q in range(3):
                        b = filled(act, "gate", 6 * m + 3 * gate + q)
                        width = CHUNKS[q][2]
                        last = av(ar(dst + NT * m + 384 * q, width), b[:, 0:width], ACT.Sigmoid,
                                  bias=par(bias)[:, m:m + 1])
                        done(last)
            act.wait_ge(s("lam_ready"), 1)
            act.wait_ge(emptied["act"], empties(where["gate", 23] + 1, "act"))
            for m in range(ML):
                av(ar(TG + NT * m, NT), ar(RG + NT * m, NT), ACT.Tanh, scale=lrc[:, 20 + m:21 + m]).then_inc(
                    s("tanh_ready"), 1)
            act.wait_ge(s("tanh_ready"), 4)
            for m in range(ML):
                av(ar(RG + NT * m, NT), ar(RG + NT * m, NT), ACT.Exp, scale=lrc[:, 16 + m:17 + m]).then_inc(
                    s("decay_ready"), 1)
            act.wait_ge(s("ratio_ready"), 1)
            av(ar(TG, 4352), ar(TG, 4352), ACT.Sqrt, scale=2.0).then_inc(s("root_ready"), 1)
            for q in range(8):
                b = filled(act, "k0", q)
                k0 = group(q, 0)
                done(nc.scalar.copy(ar(K0, 4096, GS).rearrange("p (g n) -> p g n", g=G)[:, k0:k0 + 7:2, :],
                                    b[0:GS, :].rearrange("p (g n) -> p g n", g=4)))
            for q in range(8):
                b = filled(act, "rt", q)
                done(nc.scalar.copy(ar(RT + 512 * q, 512), b[:, :]))
            for q in range(11):
                b = filled(act, "ug", q)
                n = 136 * (min(3 * q + 3, G) - 3 * q)
                done(nc.scalar.copy(ar(UG + 408 * q, n), b[:, 0:n]))
            for q in range(16):
                b = filled(act, "y", q)
                base, n = ((YT_, NC), (Y8_, NCS))[q // 8]
                out = ar(base, 4096, n).rearrange("p (k g i) -> p k g i", k=L, g=G)
                for e in range(4):
                    last = av(out[:, :, group(q % 8, e), :], b[0:n, P * e:P * e + P].rearrange("p (k i) -> p k i", k=L),
                              ACT.Gelu_apprx_tanh)
                done(last)
            for m in range(ML):
                for q, (k0, nk, width) in enumerate(CHUNKS):
                    b = filled(act, "glu", 3 * m + q)
                    done(av(ar(YS5 + NT * m + P * k0, width), b[:, 0:width], ACT.Sigmoid, bias=par("bglu")[:, m:m + 1]))
            act.wait_ge(s("yl_ready"), 1)
            stage_emptied(act, "gyT")
            av(ar(SQ, 4352), ar(YL, 4352), ACT.Square).then_inc(s("sq_ready"), 1)
            act.wait_ge(s("ys5_ready"), 1)
            av(ar(SQ + 4352, 4352), ar(YS5, 4352), ACT.Square).then_inc(s("sq_ready"), 1)
            act.wait_ge(s("ms2_ready"), 2)
            av(ssq[:, 0:16], ssq[:, 18:34], ACT.Sqrt).then_inc(s("rt2_ready"), 1)
            av(ssq[0:DSEQ, 16:18], ssq[0:DSEQ, 34:36], ACT.Sqrt).then_inc(s("rt2_ready"), 1)
            for t in range(NTILE):
                n = cols(t)[1]
                act.wait_ge(s("x1_ready"), t + 1)
                if t:
                    act.wait_ge(s("ssq3"), t)
                else:
                    act.wait_ge(s("ssq1"), NTILE)
                av(junk[0:n, :], ar(X1 + 1024 * t, 1024, n), ACT.Square, accum_out=rms3[0:n, t:t + 1]).then_inc(
                    s("ssq3"), 1)
            act.wait_ge(s("ms3_ready"), 2)
            av(rms3[:, 20:28], rms3[:, 10:18], ACT.Sqrt).then_inc(s("rt3_ready"), 1)
            av(rms3[0:DSEQ, 28:29], rms3[0:DSEQ, 18:19], ACT.Sqrt).then_inc(s("rt3_ready"), 1)
            act.wait_ge(s("a2_ready"), 1)
            modulated(act, "act", "h2T", H2T, a2, 24)

            act.wait_ge(s("keys_in"), 16)

            def head_moves(h, first):
                if not first:
                    act.wait_ge(s("s_full"), 2 * h)
                nc.scalar.copy(ar(WK, 256), arena[:, bass.ds(256 * h + KEYS, 256)]).then_inc(s("kbuf_ready"), 1)
                for c in range(2):
                    act.wait_ge(s("q_full"), 2 * h + c + 1)
                    for q in range(3):
                        width = CHUNKS[q][2]
                        last = nc.scalar.copy(ar(QT + NT * c + 384 * q, width), ps[q][:, 0:width])
                    last.then_inc(s("q_moved"), 1)
                    act.wait_ge(s("s_full"), 2 * h + c + 1)
                    if not first:
                        act.wait_ge(s("scores_read"), 2 * h + c - 1)
                    for half in range(2):
                        nc.scalar.copy(ar(SB + 1152 * c + 512 * half, 512), ps[3 + half][:, :])
                    nc.scalar.copy(ar(SB + 1152 * c + 1024, P, DSEQ), ps[5][0:DSEQ, 0:P]).then_inc(s("s_moved"), 1)
                act.wait_ge(s("softmax_in"), h + 1)
                av(smx[:, 0:8, :], smx[:, 0:8, :], ACT.Exp)
                av(smx[0:DSEQ, 8, :], smx[0:DSEQ, 8, :], ACT.Exp).then_inc(s("softmax_exp"), 1)

            head_moves(0, True)
            with act.Fori(1, HEADS) as h:
                head_moves(h, False)

            for a in range(3):
                for q in range(3):
                    act.wait_ge(s("picksT_full"), 3 * a + q + 1)
                    width = (512, 512, DSEQ)[q]
                    nc.scalar.copy(ar(ITR + NT * a + 512 * q, width), ps[(3 * a + q) % 8][:, 0:width]).then_inc(
                        s("picksT_moved"), 1)

            def move_block(b, buf, first):
                if not first:
                    act.wait_ge(s(f"coef_out{buf}"), 8 * (b - buf))
                out = ar(CB + 8192 * buf, 8192).rearrange("p (i n) -> p n i", n=64)
                for g in range(8):
                    act.wait_ge(s("c_full"), 8 * b + g + 1)
                    for half in range(2):
                        n0 = 8 * g + 4 * half
                        nc.scalar.copy(out[:, n0:n0 + 4, :],
                                       ps[2 * (g % 4) + half][:, :].rearrange("p (n i) -> p n i", n=4)).then_inc(
                            s("c_moved"), 1)

            move_block(0, 0, True)
            move_block(1, 1, True)
            with act.Fori(1, 8) as i:
                move_block(2 * i, 0, False)
                move_block(2 * i + 1, 1, False)
            move_block(16, 0, False)

            def gelus(t, u, first):
                if not first:
                    act.wait_ge(s("v_bank_full"), 24 * (t - 1))
                for e in range(2):
                    for q, (k0, nk, width) in enumerate(CHUNKS):
                        j = 3 * e + q
                        act.wait_ge(s("s_bank_full"), 6 * t + j + 1)
                        av(ar(WB + 2176 * u + NT * e + P * k0, width), ps[(6 * u + j) % 4][:, 0:width],
                           ACT.Gelu_apprx_tanh).then_inc(s("s_gelu"), 1)

            gelus(0, 0, True)
            gelus(1, 1, True)
            with act.Fori(1, 32) as i:
                gelus(2 * i, 0, False)
                gelus(2 * i + 1, 1, False)
            for t in range(NTILE):
                n = cols(t)[1]
                act.wait_ge(s("x2_done"), t + 1)
                if t:
                    act.wait_ge(s("ssq4"), t)
                else:
                    act.wait_ge(s("ssq3"), NTILE)
                av(junk[0:n, :], ar(XL + 1024 * t, 1024, n), ACT.Square, accum_out=rms4[0:n, t:t + 1]).then_inc(
                    s("ssq4"), 1)
            act.wait_ge(s("ms4_ready"), 2)
            av(rms4[:, 20:28], rms4[:, 10:18], ACT.Sqrt).then_inc(s("rt4_ready"), 1)
            av(rms4[0:DSEQ, 28:29], rms4[0:DSEQ, 18:19], ACT.Sqrt).then_inc(s("rt4_ready"), 1)

        @block.vector
        def _(dve):
            V = nc.vector
            chain = [0]

            def link(ins):
                chain[0] += 1
                ins.then_inc(s("dve_chain"), 1)
                dve.wait_ge(s("dve_chain"), chain[0])

            def tt(o, a, b, op):
                return V.tensor_tensor(o, a, b, op)

            def ts(o, a, x, y, op0, op1=None):
                return V.tensor_scalar(o, a, x, y, op0, op1) if op1 is not None else V.tensor_scalar(o, a, x, None, op0)

            done = lambda ins: ins.then_inc(emptied["dve"], 1)
            C = lambda i: s5c[:, i, :]
            dve.wait_ge(s("csig_ready"), 1)
            tt(csil[:, :], csil[:, :], par("cT"), ALU.mult).then_inc(s("csil_ready"), 1)
            dve.wait_ge(s("s5_dt_ready"), 1)
            tt(C(1), C(0), par("are"), ALU.mult).then_inc(s("s5_lrdt_ready"), 1)
            link(tt(C(2), C(0), par("aim"), ALU.mult))
            link(ts(lrc[:, 16:20], par("lam"), -1.0, None, ALU.mult))
            tt(lrc[:, 0:4], par("lam"), lrc[:, 16:20], ALU.max).then_inc(s("lam_abs_ready"), 1)
            dve.wait_ge(s("lam_exp_ready"), 1)
            ts(lrc[:, 8:12], lrc[:, 4:8], 1.0, None, ALU.add).then_inc(s("lam_w_ready"), 1)
            dve.wait_ge(s("lam_w_ready"), 1)
            link(ts(lrc[:, 20:24], lrc[:, 8:12], 1.0, None, ALU.is_equal))
            dve.wait_ge(s("lam_ln_ready"), 1)
            link(ts(lrc[:, 8:12], lrc[:, 8:12], -1.0, None, ALU.add))
            link(tt(lrc[:, 8:12], lrc[:, 8:12], lrc[:, 20:24], ALU.add))
            link(V.reciprocal(lrc[:, 8:12], lrc[:, 8:12]))
            link(tt(lrc[:, 12:16], lrc[:, 12:16], lrc[:, 20:24], ALU.add))
            link(tt(lrc[:, 12:16], lrc[:, 12:16], lrc[:, 4:8], ALU.mult))
            link(tt(lrc[:, 12:16], lrc[:, 12:16], lrc[:, 8:12], ALU.mult))
            link(ts(lrc[:, 16:20], lrc[:, 16:20], 0.0, None, ALU.max))
            link(tt(lrc[:, 12:16], lrc[:, 12:16], lrc[:, 16:20], ALU.add))
            link(ts(lrc[:, 20:24], lrc[:, 12:16], LRU_C, None, ALU.mult))
            ts(lrc[:, 16:20], lrc[:, 12:16], -LRU_C, None, ALU.mult).then_inc(s("lam_ready"), 1)
            for f in range(2):
                ph, t = C(7 + 4 * f), C(5)
                if f == 0:
                    link(V.tensor_copy(ph, C(2)))
                else:
                    link(ts(ph, C(7), float(L), None, ALU.mult))
                link(ts(t, ph, 1.0 / TWO_PI, MAGIC, ALU.mult, ALU.add))
                link(ts(t, t, -MAGIC, None, ALU.add))
                for part in (6.28125, 0.0019340515136718750, TWO_PI - 6.28125 - 0.0019340515136718750):
                    link(V.scalar_tensor_tensor(out=ph, in0=t, scalar=-part, in1=ph, op0=ALU.mult, op1=ALU.add))
                ts(ph, ph, 3.1415925, -3.1415925, ALU.min, ALU.max).then_inc(s("phase_ready"), 1)
                dve.wait_ge(s("phase_ready"), f + 1)
                dve.wait_ge(s("sin_ready"), 2 * f + 2)
                link(tt(C(10 + 4 * f), C(9 + 4 * f), C(9 + 4 * f), ALU.mult))
                link(ts(C(10 + 4 * f), C(10 + 4 * f), -2.0, 1.0, ALU.mult, ALU.add))
            dve.wait_ge(s("s5_mag_ready"), 2)
            tt(C(15), C(3), C(10), ALU.mult)
            link(tt(C(16), C(3), C(8), ALU.mult))
            lr, li = par("are"), par("aim")
            link(tt(C(17), lr, lr, ALU.mult))
            link(tt(C(18), li, li, ALU.mult))
            link(tt(C(17), C(17), C(18), ALU.add))
            link(V.reciprocal(C(17), C(17)))
            link(ts(C(18), C(15), -1.0, None, ALU.add))
            link(tt(C(19), C(18), lr, ALU.mult))
            link(tt(C(20), C(16), li, ALU.mult))
            link(tt(C(19), C(19), C(20), ALU.add))
            link(tt(C(20), C(16), lr, ALU.mult))
            link(tt(C(21), C(18), li, ALU.mult))
            link(tt(C(20), C(20), C(21), ALU.subtract))
            link(tt(C(19), C(19), C(17), ALU.mult))
            link(tt(C(20), C(20), C(17), ALU.mult))

            def b3(v, shape):
                return v.unsqueeze(2).to_broadcast(shape)

            def cmul(o_re, o_im, a_re, a_im, b_re, b_im, t1, neg=False, flag=None):
                tt(o_re, a_re, b_re, ALU.mult)
                link(tt(t1, a_im, b_im, ALU.mult))
                link(tt(o_re, o_re, t1, ALU.subtract))
                tt(o_im, a_im, b_re, ALU.mult)
                link(tt(t1, a_re, b_im, ALU.mult))
                if neg:
                    last = V.scalar_tensor_tensor(out=o_im, in0=o_im, scalar=-1.0, in1=t1, op0=ALU.mult,
                                                  op1=ALU.subtract)
                else:
                    last = tt(o_im, o_im, t1, ALU.add)
                if flag:
                    last.then_inc(s(flag), 1)
                    dve.wait_ge(s(flag), 1)
                else:
                    link(last)

            q3 = lambda v: v.rearrange("p (a i) -> p a i", a=PAIRS)
            sh = [P, PAIRS, GS]
            cmul(q3(bb[:, 0, :]), q3(bb[:, 1, :]), q3(par("bre")), q3(par("bim")), b3(C(19), sh), b3(C(20), sh),
                 q3(tmp256))
            link(V.memset(pw[:, 0, :, 0:1], 1.0))
            link(V.memset(pw[:, 1, :, 0:1], 0.0))
            link(V.tensor_copy(pw[:, 0, :, 1], C(15)))
            link(V.tensor_copy(pw[:, 1, :, 1], C(16)))
            for m in (1, 2, 4):
                shp = [P, PAIRS, m]
                cmul(pw[:, 0, :, m + 1:2 * m + 1], pw[:, 1, :, m + 1:2 * m + 1], pw[:, 0, :, 1:m + 1],
                     pw[:, 1, :, 1:m + 1], pw[:, 0, :, m:m + 1].to_broadcast(shp),
                     pw[:, 1, :, m:m + 1].to_broadcast(shp), tmp256[:, 0:PAIRS * m].rearrange("p (a m) -> p a m", m=m))
            for k in range(L):
                link(V.tensor_copy(pwr[:, :, :, k], pw[:, :, :, L - 1 - k]))

            for n in range(12):
                b = filled(dve, "mod", n)
                if n == 0:
                    dve.wait_ge(s("b_ada_in"), 16)
                done(tt(ar(MROW + 512 * n, 512, 2), b[0:2, :], ar(BROW + 512 * n, 512, 2), ALU.add))
            stage_emptied(dve, "modT")

            def one_plus(dst, sc0, norm, name):
                link(ts(dst[:, :, :], mcol[:, sc0:sc0 + 8, :], 1.0, None, ALU.add))
                tt(dst[:, :, :], dst[:, :, :], par(norm).unsqueeze(2).to_broadcast([P, 8, 2]), ALU.mult).then_inc(
                    s(name), 1)

            one_plus(a1, 8, "norm1", "a1_ready")
            one_plus(a2, 32, "norm2", "a2_ready")
            dve.wait_ge(s("ssq1"), NTILE)

            def rnorm(src, mid, root, n8, ns, width, ms, rt):
                ts(mid[:, 0:n8], src[:, 0:n8], 1.0 / width, EPS, ALU.mult, ALU.add).then_inc(s(ms), 1)
                ts(mid[0:DSEQ, n8:n8 + ns], src[0:DSEQ, n8:n8 + ns], 1.0 / width, EPS, ALU.mult, ALU.add).then_inc(
                    s(ms), 1)
                dve.wait_ge(s(rt), 2)
                link(V.reciprocal(root[:, 0:n8], root[:, 0:n8]))
                link(V.reciprocal(root[0:DSEQ, n8:n8 + ns], root[0:DSEQ, n8:n8 + ns]))

            rnorm(ssq[:, 0:9], ssq[:, 9:18], ssq[:, 18:27], 8, 1, DM, "ms1_ready", "rt1_ready")
            for t in range(NTILE):
                n = cols(t)[1]
                ts(ar(XN + 1024 * t, 1024, n), ar(X0 + 1024 * t, 1024, n), ssq[0:n, 18 + t:19 + t], None,
                   ALU.mult).then_inc(s("xn_ready"), 1)
            stage_emptied(dve, "g1")
            dve.wait_ge(s("a1_ready"), 1)
            modulated(dve, "dve", "h1T", HT, a1, 0)
            stage_emptied(dve, "h1T")
            for m in range(ML):
                link(V.memset(ar(XAP + 1027 * m, 3), 0.0))
                link(V.tensor_copy(ar(XAS + 67 * m, 3), par("cache")[:, 3 * m:3 * m + 3]))
            for m in range(ML):
                for q, (k0, nk, width) in enumerate(CHUNKS):
                    b = filled(dve, "z", 3 * m + q)
                    out = ar(XAP + 1027 * m + 3, SEQ).rearrange("p (c k) -> p k c", k=L)[:, k0:k0 + nk, :]
                    last = V.tensor_copy(out, b[:, 0:P * nk].rearrange("p (k c) -> p k c", k=nk))
                    if q == 2:
                        out = ar(XAS + 67 * m + 3, DSEQ).rearrange("p (c k) -> p k c", k=L)
                        last = V.tensor_copy(out, b[:, 256:320].rearrange("p (k c) -> p k c", k=L))
                    done(last)
            dve.wait_ge(bank_full, where["us", 8] + 1)
            stage_emptied(dve, "z", 12)
            for m in range(ML):
                for dst, src, n in ((XC + NT * m, XAP + 1027 * m, SEQ), (XC + NT * m + SEQ, XAS + 67 * m, DSEQ)):
                    w = par("conv_w")
                    link(ts(ar(dst, n), ar(src + 3, n), w[:, 4 * m + 3:4 * m + 4], par("conv_b")[:, m:m + 1],
                            ALU.mult, ALU.add))
                    for k in range(3):
                        last = V.scalar_tensor_tensor(out=ar(dst, n), in0=ar(src + k, n),
                                                      scalar=w[:, 4 * m + k:4 * m + k + 1], in1=ar(dst, n),
                                                      op0=ALU.mult, op1=ALU.add)
                        if k < 2:
                            link(last)
                    last.then_inc(s("xc_ready"), 1)
            dve.wait_ge(s("xc_ready"), 8)
            stage_emptied(dve, "gate")
            link(tt(ar(IG, 4352), ar(IG, 4352), ar(XC, 4352), ALU.mult))
            dve.wait_ge(s("tanh_ready"), 4)
            link(ts(ar(HS, 4352), ar(TG, 4352), 1.0, None, ALU.add))
            link(V.reciprocal(ar(HS, 4352), ar(HS, 4352)))
            tt(ar(TG, 4352), ar(TG, 4352), ar(HS, 4352), ALU.mult).then_inc(s("ratio_ready"), 1)
            dve.wait_ge(s("root_ready"), 1)
            link(tt(ar(IG, 4352), ar(IG, 4352), ar(TG, 4352), ALU.mult))
            dve.wait_ge(s("decay_ready"), 4)
            for m in range(ML):
                o = NT * m
                V.tensor_tensor_scan(ar(HS + o, SEQ), ar(RG + o, SEQ), ar(IG + o, SEQ), 0.0, ALU.mult, ALU.add)
                link(V.tensor_tensor_scan(ar(HS + o + SEQ, DSEQ), ar(RG + o + SEQ, DSEQ), ar(IG + o + SEQ, DSEQ),
                                          par("h0")[:, m:m + 1], ALU.mult, ALU.add))
                V.tensor_copy(fin[:, 64 + m:65 + m], ar(HS + o + SEQ - 1, 1))
                last = V.tensor_copy(fin[:, 68 + m:69 + m], ar(HS + o + NT - 1, 1))
                if m == ML - 1:
                    last.then_inc(s("fin_ready"), 1)
                tk = lambda off, n: ar(off, n).rearrange("p (c k) -> p k c", k=L)
                ct = lambda off, n: ar(off, n).rearrange("p (k c) -> p k c", k=L)
                tt(ct(YL + o, SEQ), tk(HS + o, SEQ), tk(GA + o, SEQ), ALU.mult)
                last = tt(ct(YL + o + SEQ, DSEQ), tk(HS + o + SEQ, DSEQ), tk(GA + o + SEQ, DSEQ), ALU.mult)
            last.then_inc(s("yl_ready"), 1)
            dve.wait_ge(s("yl_ready"), 1)
            dve.wait_ge(s("states_out"), 16 * 8)
            sh4 = [P, PAIRS, 9, GS]
            f4 = lambda off, k: ar(off, PAIRS * k * GS).rearrange("p (a k i) -> p a k i", a=PAIRS, k=k)
            dup = lambda v, k: q3(v).unsqueeze(2).to_broadcast([P, PAIRS, k, GS])
            pb = lambda v, k: v.unsqueeze(3).to_broadcast([P, PAIRS, k, GS])
            dve.wait_ge(bank_full, where["gate", 23] + 1)
            cmul(f4(OC, 9), f4(OC + 2304, 9), dup(par("cre"), 9), dup(par("cim"), 9), pb(pw[:, 0], 9), pb(pw[:, 1], 9),
                 f4(TMP, 9), neg=True, flag="oc_ready")
            cmul(f4(XR, 8), f4(XR + 2048, 8), dup(bb[:, 0, :], 8), dup(bb[:, 1, :], 8), pb(pwr[:, 0], 8),
                 pb(pwr[:, 1], 8), f4(TMP, 8), flag="xr_ready")
            V.memset(ar(TT, 4096), 0.0).then_inc(s("t_zeroed"), 1)
            stage_emptied(dve, "k0")
            dd = ddg.rearrange("p (g i) -> p g i", g=G)
            link(tt(dd, dd, ident[0:GS, 0:GS].unsqueeze(1).to_broadcast([GS, G, GS]), ALU.mult))
            kb = ar(K0, 4096, GS).rearrange("p (g n) -> p g n", g=G)[:, :, 0:GS]
            tt(kb, kb, dd, ALU.add).then_inc(s("k0_ready"), 1)
            stage_emptied(dve, "ug")
            E = [ar(EE + SFLAT * r, SFLAT).rearrange("p (a n) -> p a n", a=PAIRS) for r in range(2)]
            for r, v, c in ((0, 1.0, 14), (1, 0.0, 12)):
                link(V.memset(E[r][:, :, 0:1], v))
                link(V.tensor_copy(E[r][:, :, 1], C(c)))
            for m in (1, 2, 4, 8, 16, 32, 64):
                shp = [P, PAIRS, m]
                cmul(E[0][:, :, m + 1:2 * m + 1], E[1][:, :, m + 1:2 * m + 1], E[0][:, :, 1:m + 1],
                     E[1][:, :, 1:m + 1], E[0][:, :, m:m + 1].to_broadcast(shp), E[1][:, :, m:m + 1].to_broadcast(shp),
                     ar(TMP, PAIRS * m).rearrange("p (a m) -> p a m", m=m))
            for r in range(2):
                link(V.tensor_copy(E[r][:, :, NC + 1:SLOTS], E[r][:, :, 0:NCS + 1]))
            dve.wait_ge(s("toeplitz_in"), 16 * L)
            md = ar(MD, SFLAT).rearrange("p (a n) -> p a n", a=PAIRS)
            link(V.tensor_copy(md, C(4).unsqueeze(2).to_broadcast([P, PAIRS, SLOTS])))
            link(V.memset(md[:, :, 0:1], 0.0))
            link(V.memset(md[:, :, NC + 1:NC + 2], 0.0))
            vs = [ar(VV + SFLAT * r, SFLAT).rearrange("p (a n) -> p a n", a=PAIRS) for r in range(2)]
            stage_emptied(dve, "rt")
            for a in range(PAIRS):
                b = filled(dve, "v", a)
                for r in range(2):
                    V.tensor_copy(vs[r][:, a, 1:NC + 1], b[:, 136 * r:136 * r + P])
                    last = V.tensor_copy(vs[r][:, a, NC + 2:SLOTS], b[:, 136 * r + P:136 * r + 136])
                done(last)
            for r, name in enumerate(("s0re", "s0im")):
                link(V.memset(vs[r][:, :, 0:1], 0.0))
                link(V.tensor_copy(vs[r][:, :, NC + 1], par(name)))
            stage_emptied(dve, "v")
            ev, od = [ar(EE + SFLAT * r, SFLAT) for r in range(2)], [ar(VV + SFLAT * r, SFLAT) for r in range(2)]
            t1, t2 = ar(TMP, SFLAT), ar(TMP + SFLAT, SFLAT)

            tt(t1, od[0], ev[1], ALU.mult)
            link(tt(t2, od[1], ev[1], ALU.mult))
            tt(od[0], od[0], ev[0], ALU.mult)
            link(tt(od[1], od[1], ev[0], ALU.mult))
            tt(od[0], od[0], t2, ALU.add)
            link(tt(od[1], od[1], t1, ALU.subtract))
            V.tensor_tensor_scan(t1, ar(MD, SFLAT), od[0], 0.0, ALU.mult, ALU.add)
            link(V.tensor_tensor_scan(t2, ar(MD, SFLAT), od[1], 0.0, ALU.mult, ALU.add))
            tt(od[0], t1, ev[0], ALU.mult)
            tt(od[1], t1, ev[1], ALU.mult)
            link(tt(ar(MD, SFLAT), t2, ev[1], ALU.mult))
            link(tt(t2, t2, ev[0], ALU.mult))
            tt(od[0], od[0], ar(MD, SFLAT), ALU.subtract)
            tt(od[1], od[1], t2, ALU.add).then_inc(s("state_ready"), 1)
            dve.wait_ge(s("state_ready"), 1)
            for r in range(2):
                V.tensor_copy(fin[:, 16 * r:16 * r + 16], vs[r][:, :, NC])
                last = V.tensor_copy(fin[:, 32 + 16 * r:48 + 16 * r], vs[r][:, :, SLOTS - 1])
            last.then_inc(s("fin_ready"), 1)
            for j in range(4):
                for q in range(3):
                    b = filled(dve, "gyT", 3 * j + q)
                    width = 512 if q < 2 else DSEQ
                    done(V.tensor_copy(ar(GYT + NT * j + 512 * q, width), b[:, 0:width]))
            stage_emptied(dve, "glu")
            tt(ar(YS5, 4352), ar(YS5, 4352), ar(GYT, 4352), ALU.mult).then_inc(s("ys5_ready"), 1)
            dve.wait_ge(s("sq_ready"), 2)
            for src, name in ((YL, "gnl"), (YS5, "gns")):
                for m in range(ML):
                    last = ts(ar(src + NT * m, NT), ar(src + NT * m, NT), par(name)[:, m:m + 1], None, ALU.mult)
                last.then_inc(s("halves_scaled"), 1)
            b = filled(dve, "rms", 0)
            for half in range(2):
                V.tensor_copy(ssq[:, 8 * half:8 * half + 8], b[:, 9 * half:9 * half + 8])
                last = V.tensor_copy(ssq[0:DSEQ, 16 + half:17 + half], b[0:DSEQ, 9 * half + 8:9 * half + 9])
            done(last)
            stage_emptied(dve, "rms")
            rnorm(ssq[:, 0:18], ssq[:, 18:36], ssq[:, 0:18], 16, 2, DL, "ms2_ready", "rt2_ready")
            dve.wait_ge(s("x_again_in"), 32)
            for t in range(NTILE):
                n, g = cols(t)[1], t // 8
                for nh in range(2):
                    m0, m1 = ar(MT + 512 * nh, 512, n), ar(X1 + 1024 * t + 512 * nh, 512, n)
                    rl = ssq[0:n, t:t + 1] if t < 8 else ssq[0:n, 16:17]
                    rs = ssq[0:n, 8 + t:9 + t] if t < 8 else ssq[0:n, 17:18]
                    b = filled(dve, "mix", 4 * t + 2 * nh)
                    done(ts(m0, b[0:n, :], rl, None, ALU.mult))
                    dve.wait_ge(emptied["dve"], empties(where["mix", 4 * t + 2 * nh] + 1, "dve"))
                    b = filled(dve, "mix", 4 * t + 2 * nh + 1)
                    done(V.scalar_tensor_tensor(out=m0, in0=b[0:n, :], scalar=rs, in1=m0, op0=ALU.mult, op1=ALU.add))
                    dve.wait_ge(emptied["dve"], empties(where["mix", 4 * t + 2 * nh + 1] + 1, "dve"))
                    link(tt(m0, m0, ar(G1B + 1024 * g + 512 * nh, 512, n), ALU.mult))
                    last = tt(m1, m1, m0, ALU.add)
                    if nh == 0:
                        link(last)
                last.then_inc(s("x1_ready"), 1)
            dve.wait_ge(s("ssq3"), NTILE)
            rnorm(rms3[:, 0:9], rms3[:, 10:19], rms3[:, 20:29], 8, 1, DM, "ms3_ready", "rt3_ready")
            for t in range(NTILE):
                n = cols(t)[1]
                ts(ar(XN2 + 1024 * t, 1024, n), ar(X1 + 1024 * t, 1024, n), rms3[0:n, 20 + t:21 + t], None,
                   ALU.mult).then_inc(s("xn2_ready"), 1)
            dve.wait_ge(s("a2_ready"), 1)
            modulated(dve, "dve", "h2T", H2T, a2, 24)
            stage_emptied(dve, "h2T")
            dve.wait_ge(s("x1_out"), 32)

            def head_picks(h):
                cnt = [0]

                def lk(ins):
                    cnt[0] += 1
                    ins.then_inc(s("pick_chain"), 1)
                    dve.wait_ge(s("pick_chain"), NLINK * h + cnt[0])

                def top16(scores, width, vals, idx):
                    rest = lambda t, n: ar(CW2 + width * t, width, n)
                    for half, src in ((0, scores), (1, rest)):
                        e = slice(8 * half, 8 * half + 8)
                        V.memset(mark[:, :], 0.0)
                        for t in range(NTILE):
                            n = cols(t)[1]
                            last = V.max(vals[0:n, t, e], src(t, n))
                        lk(last)
                        V.memset(mark[:, :], 0.0)
                        for t in range(NTILE):
                            n = cols(t)[1]
                            last = V.max_index(idx[0:n, t, e], vals[0:n, t, e], src(t, n))
                            if half == 0:
                                last = V.match_replace(rest(t, n), vals[0:n, t, e], src(t, n), NEG)
                        lk(last)

                for c in range(2):
                    dve.wait_ge(s("s_moved"), 2 * h + c + 1)
                    top16(lambda t, n: ar(SB + 1152 * c + P * t, P, n), P, vtop[:, c], itop[:, c])
                    V.tensor_copy(itf[:, c, 0:8, :], itop[:, c, 0:8, :])
                    V.tensor_copy(itf[0:DSEQ, c, 8, :], itop[0:DSEQ, c, 8, :]).then_inc(s("scores_read"), 1)
                for n, t0, nt in ((P, 0, 8), (DSEQ, 8, 1)):
                    lk(tt(ar(CAND + 256 * t0, 256 * nt, n).rearrange("p (t a b) -> p t a b", t=nt, a=TOPK),
                          vtop[0:n, 0, t0:t0 + nt, :].unsqueeze(3).to_broadcast([n, nt, TOPK, TOPK]),
                          vtop[0:n, 1, t0:t0 + nt, :].unsqueeze(2).to_broadcast([n, nt, TOPK, TOPK]), ALU.add))
                top16(lambda t, n: ar(CAND + 256 * t, 256, n), 256, smx, pos)
                for n, t0, nt in ((P, 0, 8), (DSEQ, 8, 1)):
                    lk(V.tensor_copy(mx1[0:n, t0:t0 + nt, :], smx[0:n, t0:t0 + nt, 0:1]))
                for n, t0, nt in ((P, 0, 8), (DSEQ, 8, 1)):
                    v = smx[0:n, t0:t0 + nt, :]
                    last = tt(v, v, mx1[0:n, t0:t0 + nt, :].to_broadcast([n, nt, TOPK]), ALU.subtract)
                    if t0 == 0:
                        lk(last)
                last.then_inc(s("softmax_in"), 1)
                for n, t0, nt in ((P, 0, 8), (DSEQ, 8, 1)):
                    pv = pos[0:n, t0:t0 + nt, :]
                    ts(posab[0:n, 0, t0:t0 + nt, :], pv, 4, None, ALU.logical_shift_right)
                    lk(ts(posab[0:n, 1, t0:t0 + nt, :], pv, 15, None, ALU.bitwise_and))
                    lk(V.tensor_copy(pf[0:n, :, t0:t0 + nt, :], posab[0:n, :, t0:t0 + nt, :]))
                for c in range(2):
                    for n, t0, nt in ((P, 0, 8), (DSEQ, 8, 1)):
                        v = ar(D1 + 256 * t0, 256 * nt, n)
                        v4 = v.rearrange("p (t j a) -> p t j a", t=nt, j=TOPK)
                        shp = [n, nt, TOPK, TOPK]
                        i16 = iota[0:n, 0:TOPK].unsqueeze(1).unsqueeze(1).to_broadcast(shp)
                        lk(tt(v4, pf[0:n, c, t0:t0 + nt, :].unsqueeze(3).to_broadcast(shp), i16, ALU.is_equal))
                        lk(tt(v4, v4, itf[0:n, c, t0:t0 + nt, :].unsqueeze(2).to_broadcast(shp), ALU.mult))
                        lk(V.tensor_reduce(pick[0:n, t0:t0 + nt, :], v4, AX.X, ALU.add))
                    for n, t0, nt in ((P, 0, 8), (DSEQ, 8, 1)):
                        lk(V.tensor_copy(iall(c, n, t0, nt, h), pick[0:n, t0:t0 + nt, :]))
                dve.wait_ge(s("softmax_exp"), h + 1)
                for n, t0, nt in ((P, 0, 8), (DSEQ, 8, 1)):
                    lk(V.tensor_reduce(mx1[0:n, t0:t0 + nt, :].rearrange("p t o -> p (t o)"), smx[0:n, t0:t0 + nt, :],
                                       AX.X, ALU.add))
                    lk(V.reciprocal(mx1[0:n, t0:t0 + nt, :], mx1[0:n, t0:t0 + nt, :]))
                    last = tt(iall(2, n, t0, nt, h), smx[0:n, t0:t0 + nt, :],
                              mx1[0:n, t0:t0 + nt, :].to_broadcast([n, nt, TOPK]), ALU.mult)
                last.then_inc(s("picks_ready"), 1)
                dve.wait_ge(s("picks_ready"), h + 1)
                return cnt[0]

            def iall(a, n, t0, nt, h):
                v = ar(IALL + 1152 * a + P * t0, P * nt, n).rearrange("p (t j) -> p t j", t=nt)
                return v[:, :, bass.ds(TOPK * h, TOPK)]

            with dve.Fori(0, HEADS) as h:
                got = head_picks(h)
            assert got == NLINK, got

            dve.wait_ge(s("picksT_moved"), 9)

            def onehots(b, first):
                for g in range(8):
                    if not (first and g < 2):
                        dve.wait_ge(s("c_full"), 8 * b + g - 1)
                    for a, dst in ((0, PB), (1, QB)):
                        for j in range(8):
                            idx = itc(a, b, 8 * g + j)
                            out = ar(dst + 1024 * (g % 2) + P * j, P)
                            if a == 0:
                                last = ts(out, iota[:, :], idx, None, ALU.is_equal)
                            else:
                                last = ts(out, iota[:, :], idx, itc(2, b, 8 * g + j), ALU.is_equal, ALU.mult)
                        last.then_inc(s("onehot_ready"), 1)

            def itc(a, b, n):
                return arena[:, bass.ds(ITR + NT * a + 64 * b + n, 1)]

            onehots(0, True)
            onehots(1, False)
            with dve.Fori(1, 8) as i:
                onehots(2 * i, False)
                onehots(2 * i + 1, False)
            onehots(16, False)
            dve.wait_ge(s("coef_out0"), 16 * 9)
            dve.wait_ge(s("coef_out1"), 16 * 8)
            V.memset(ar(YB, 8704), 0.0).then_inc(s("y_clear"), 1)
            dve.wait_ge(s("y_clear"), 1)

            def weigh(t, u, i):
                dve.wait_ge(s(f"c_in{u}"), 16 * i + 16)
                for e in range(2):
                    for q, (k0, nk, width) in enumerate(CHUNKS):
                        dve.wait_ge(s("s_gelu"), 6 * t + 3 * e + q + 1)
                        w = ar(WB + 2176 * u + NT * e + P * k0, width).rearrange("p (b n) -> p b n", n=64)
                        c = ar(CBD + 2176 * u, 2176).rearrange("p (b e n) -> p b e n", b=17, e=2)[
                            :, 2 * k0:2 * k0 + width // 64, e, :]
                        tt(w, w, c, ALU.mult).then_inc(s("w_ready"), 1)

            def add_up(t, first):
                if not first:
                    dve.wait_ge(s("y_added"), 24 * t)
                for d in range(8):
                    for q, (k0, nk, width) in enumerate(CHUNKS):
                        j = 3 * d + q
                        dve.wait_ge(s("v_bank_full"), 24 * t + j + 1)
                        y = ar(YB + NT * d + P * k0, width)
                        tt(y, ps[4 + j % 4][:, 0:width], y, ALU.add).then_inc(s("y_added"), 1)

            weigh(0, 0, 0)
            weigh(1, 1, 0)
            add_up(0, True)
            with dve.Fori(1, 32) as i:
                weigh(2 * i, 0, i)
                add_up(2 * i - 1, False)
                weigh(2 * i + 1, 1, i)
                add_up(2 * i, False)
            add_up(63, False)
            dve.wait_ge(s("y_added"), 24 * 64)
            for d in range(8):
                ts(ar(YB + NT * d, SEQ), ar(YB + NT * d, SEQ), mcol[:, 40 + d, 0:1], None, ALU.mult)
                last = ts(ar(YB + NT * d + SEQ, DSEQ), ar(YB + NT * d + SEQ, DSEQ), mcol[:, 40 + d, 1:2], None, ALU.mult)
            last.then_inc(s("y_scaled"), 1)
            dve.wait_ge(s("x1_back"), 32)
            for t in range(NTILE):
                n = cols(t)[1]
                dve.wait_ge(s("yT_full"), t + 1)
                for half in range(2):
                    x = ar(XL + 1024 * t + 512 * half, 512, n)
                    last = tt(x, ps[2 * (t % 4) + half][0:n, :], x, ALU.add)
                    if half == 0:
                        link(last)
                last.then_inc(s("x2_done"), 1)
            dve.wait_ge(s("ssq4"), NTILE)
            rnorm(rms4[:, 0:9], rms4[:, 10:19], rms4[:, 20:29], 8, 1, DM, "ms4_ready", "rt4_ready")
            dve.wait_ge(s("norm_f_in"), 16)
            for t in range(NTILE):
                n = cols(t)[1]
                x = ar(XL + 1024 * t, 1024, n)
                V.scalar_tensor_tensor(out=x, in0=x, scalar=rms4[0:n, 20 + t:21 + t], in1=ar(NF, 1024, n),
                                       op0=ALU.mult, op1=ALU.mult).then_inc(s("y_ready"), 1)


_ROWS = {"pack": (P, NPACK), "b_ada": (2, 6 * DM), "ddiag": (GS, DL), "w_ada": (DM, 6 * DM), "xp": (P, L, DM),
         "xs": (DSEQ, DM), "w_in": (DM, DIN), "w_glu": (DL, DL), "w_out": (DM, DM), "keys": (P, 2048),
         "wq": (HEADS, P, 2048), "ut": (64, P, 2048), "vt": (64, P, 2048), "norm_f": (P, DM)}
_OUTS = {"yp": (P, L, DM), "ys": (DSEQ, DM), "conv_p": (P, ML, 3), "conv_s": (P, ML, 3), "fin": (P, 72)}


def kernel(**inputs):
    import numpy as np
    import concourse.bacc as bacc
    from concourse.bass_utils import run_bass_kernel_spmd as run

    v = {k: np.asarray(a) for k, a in inputs.items()}

    def chan(a):
        return a.reshape(a.shape[0], -1, P).transpose(2, 1, 0)

    def pairs(a):
        a = a.reshape((PAIRS, 2, SP) + a.shape[2:])
        return np.moveaxis(a, 0, 2).reshape((P, PAIRS) + a.shape[3:])

    def heads(a):
        out = np.zeros((P, ML, P), a.dtype)
        for h in range(8):
            o = 64 * (h % 2)
            out[o:o + 64, h // 2, o:o + 64] = a[h]
        return out

    cols = {
        "cT": chan(np.concatenate([v["c_prompt"], v["c_sample"]])), "norm1": chan(v["norm1"]),
        "norm2": chan(v["norm2"]), "conv_w": chan(v["conv_w"][0]), "conv_b": chan(v["conv_b"]),
        "ba": chan(v["lru_ba"]), "bx": chan(v["lru_bx"]), "lam": chan(v["lru_lam"]), "bglu": chan(v["s5_b_glu"]),
        "gnl": chan(v["gn_lru"]), "gns": chan(v["gn_s5"]), "h0": chan(v["state_lru"][0]),
        "cache": chan(v["cache_conv"][0, 0]), "are": pairs(v["s5_a_re"][0]), "aim": pairs(v["s5_a_im"][0]),
        "ldt": pairs(np.broadcast_to(v["s5_log_dt"][0][:, None], (G, SP))),
        "s0re": pairs(v["state_s5_re"][0, 0]), "s0im": pairs(v["state_s5_im"][0, 0]),
        "bre": pairs(v["s5_b_re"][0]), "bim": pairs(v["s5_b_im"][0]),
        "cre": pairs(v["s5_c_re"][0].transpose(0, 2, 1)), "cim": pairs(v["s5_c_im"][0].transpose(0, 2, 1)),
        "wa": heads(v["lru_wa"][0]), "wx": heads(v["lru_wx"][0]),
    }
    data = {
        "pack": np.concatenate([cols[n].reshape(P, -1) for n in PACK], axis=1),
        "b_ada": np.broadcast_to(v["b_ada"], (2, 6 * DM)),
        "ddiag": np.broadcast_to(v["s5_d"], (GS, DL)),
        "w_ada": v["w_ada"][0],
        "xp": v["x_prompt"][0].reshape(P, L, DM),
        "xs": v["x_sample"][0].reshape(NCS, L, DM).transpose(1, 0, 2).reshape(DSEQ, DM),
        "w_in": v["w_in"][0], "w_glu": v["s5_w_glu"][0], "w_out": v["w_out"][0],
        "keys": v["peer_keys"][0].transpose(3, 0, 1, 2).reshape(P, 2048),
        "wq": v["peer_wq"][0].reshape(DK, P, HEADS, 2, P).transpose(2, 1, 3, 0, 4).reshape(HEADS, P, 2048),
        "ut": v["peer_u"][0].reshape(P, 64, 2, DK, P).transpose(1, 4, 2, 3, 0).reshape(64, P, 2048),
        "vt": v["peer_v"][0].reshape(P, 64, 2, DM).transpose(1, 0, 2, 3).reshape(64, P, 2048),
        "norm_f": np.broadcast_to(v["norm_f"], (P, DM)),
    }
    nc = bacc.Bacc("TRN2", target_bir_lowering=False, num_devices=1)
    A, O, arrays = {}, {}, {}
    for name, shape in _ROWS.items():
        arrays[f"in_{name}"] = np.ascontiguousarray(data[name])
        assert arrays[f"in_{name}"].shape == shape, (name, arrays[f"in_{name}"].shape)
        A[name] = nc.dram_tensor(f"in_{name}", shape, F32, kind="ExternalInput").ap()
    for name, shape in _OUTS.items():
        O[name] = nc.dram_tensor(f"out_{name}", shape, F32, kind="ExternalOutput").ap()
    trunk(nc, A, O)
    r = run(nc, [arrays], core_ids=[0]).results[0]
    yp = r["out_yp"].reshape(1, SEQ, DM)
    ys = r["out_ys"].reshape(L, NCS, DM).transpose(1, 0, 2).reshape(1, DSEQ, DM)
    conv = [r[f"out_{n}"].transpose(2, 1, 0).reshape(1, 1, 3, DL) for n in ("conv_p", "conv_s")]
    f = r["out_fin"]

    def s5(o):
        return f[:, o:o + 16].reshape(2, SP, PAIRS).transpose(2, 0, 1).reshape(1, 1, G, SP)

    lru = [f[:, o:o + 4].T.reshape(1, 1, DL) for o in (64, 68)]
    return tuple(np.ascontiguousarray(a) for a in
                 (yp, ys, conv[0], lru[0], s5(0), s5(16), conv[1], lru[1], s5(32), s5(48)))
```

```python
from contextlib import ExitStack

import concourse.bass as bass
from concourse import mybir

F32 = mybir.dt.float32
F32R = mybir.dt.float32r
U32 = mybir.dt.uint32
ALU = mybir.AluOpType
ACT = mybir.ActivationFunctionType
AX = mybir.AxisListType

P = 128
DM = 1024
DK = DM // P
SEQ, DSEQ = 1024, 64
NT = SEQ + DSEQ
L = 8
NC, NCS = SEQ // L, DSEQ // L
DL = 512
ML = DL // P
DIN = 3 * DL
CW = 4
LRU_C = 8.0
G, GS, SP = 32, 16, 64
PAIRS = G // 2
HEADS, TOPK, NKEYS = 8, 16, 128
NTILE = 9
EPS = 1e-6
SLOTS = NC + 1 + NCS + 1
SFLAT = PAIRS * SLOTS
CHUNKS = [(0, 3, 384), (3, 3, 384), (6, 2, 320)]
TWO_PI = 6.283185307179586
MAGIC = 12582912.0
NEG = -3.0e38
NLINK = 20
NCAND = 4 * 16 + 12 * 4

PACK = {}
_at = 0
for _n, _w in (("cT", 16), ("norm1", 8), ("norm2", 8), ("conv_w", 16), ("conv_b", 4), ("ba", 4), ("bx", 4),
               ("lam", 4), ("bglu", 4), ("gnl", 4), ("gns", 4), ("h0", 4), ("cache", 12), ("are", 16), ("aim", 16),
               ("ldt", 16), ("s0re", 16), ("s0im", 16), ("bre", 256), ("bim", 256), ("cre", 256), ("cim", 256),
               ("wa", 512), ("wx", 512)):
    PACK[_n] = (_at, _at + _w)
    _at += _w
NPACK = _at

ARENA = 49900
X0 = 0
XN = 9216
WADA = 9216
WIN = 18432
MROW, BROW = 30720, 36864
HT = 30720
XAP, XAS, GA = 9216, 13324, 13824
UT_, US_, U8_ = 0, 4096, 4608
XC, RG, IG, TG, HS = 39424, 22784, 27136, 31488, 35840
YL = 40192
OC, XR, TMP, RT, UG, TT, K0 = 9216, 18432, 18240, 22848, 26944, 35840, 31488
VV, MD, EE = 13824, K0, 0
YT_, YS_, Y8_ = 0, 4096, 4608
GYT, YS5, WGLU, WOUT, X1, MT, SQ = 9216, 13568, 17920, 19968, 28160, 37376, 0
XN2, H2T = 0, 9216
G1B = 46852
JUNK0, BBW, PWW, PWR, DDG, SEL = 43008, 45000, 45512, 45800, 46056, 46568
TMP256, TMP1152 = 44544, 43776
IALL, PICK, WQ, KEYS, QT, SB, WK = 17920, 21376, 27136, 31232, 33280, 35456, 37760
CAND, CW2, D1, D0, JUNK3 = 38016, 40320, 42624, 44928, 38400
PQ, CB, ITR = 22016, 30208, 46592
HHI, HLO, UR, UH, VR, VH, CBD, WR, WH, YB = 0, H2T, 17920, 19968, 22016, 26112, 30208, 32384, 36736, 41088
XL, NF, JUNK4 = 0, 10240, 12288


def trunk(nc, A, O):
    with ExitStack() as ctx:
        def sb(name, shape, dt=F32):
            return ctx.enter_context(nc.sbuf_tensor(name, shape, dt))

        def sem(name):
            return ctx.enter_context(nc.semaphore(name))

        base = nc.sbuf_base
        base += -base % 32
        arena = sb("arena", [P, ARENA])

        def placed(name, off, n):
            return nc.alloc_sbuf_tensor_at(name, [P, n], F32, offset=base + 4 * off)

        h2_buf, wq_buf = placed("h2", H2T, 8704), placed("wq", WQ, 4096)
        u_in_buf, v_in_buf, c_in_buf = placed("u_raw", UR, 2048), placed("v_raw", VR, 4096), placed("c_raw", CBD, 2176)
        w_in_buf, y_sum_buf = placed("w_raw", WR, 4352), placed("y_sum", YB, 8704)
        x1_buf, norm_f_buf, square_buf = placed("x1", XL, 9216), placed("norm_f", NF, 1024), placed("square", JUNK4, 1024)

        def rounded(name, off, n):
            return nc.alloc_sbuf_tensor_at(name, [P, n], F32R, offset=base + 4 * off)

        h_hi, h_lo = rounded("h_hi", HHI, 8704), rounded("h_lo", HLO, 8704)
        u_hi, u_lo = rounded("u_hi", UH, 2048), rounded("u_lo", UR, 2048)
        v_hi, v_lo = rounded("v_hi", VH, 4096), rounded("v_lo", VR, 4096)
        w_hi, w_lo = rounded("w_hi", WH, 4352), rounded("w_lo", WR, 4352)
        prm = sb("prm", [P, NPACK])
        ident = sb("ident", [P, P])
        ones = sb("ones", [P, 1])
        iota = sb("iota", [P, P])
        mcol = sb("mcol", [P, 48, 2])
        csil = sb("csil", [P, 16])
        a1 = sb("a1", [P, DK, 2])
        a2 = sb("a2", [P, DK, 2])
        s5c = sb("s5c", [P, 24, PAIRS])
        ssq = sb("ssq", [P, 4 * NTILE])
        lrc = sb("lrc", [P, 24])
        fin = sb("fin", [P, 72])
        rms3 = sb("rms3", [P, 30])
        rms4 = sb("rms4", [P, 30])
        ps = [ctx.enter_context(nc.psum_tensor(f"ps{i}", [P, 512], F32)) for i in range(8)]

        coef = nc.dram_tensor("coef_dram", (64, P, 17, 2, 64), F32, kind="Internal").ap()
        x1d = nc.dram_tensor("x1_dram", (P, 9216), F32, kind="Internal").ap()

        def ar(off, n, parts=P):
            return arena[0:parts, off:off + n]

        def seg(buf, off, n, parts=P):
            return buf[0:parts, off:off + n]

        def par(name, parts=P):
            return prm[0:parts, PACK[name][0]:PACK[name][1]]

        ddg = ar(DDG, DL, GS)
        sel = ar(SEL, 2 * P, 2).rearrange("p (r n) -> p r n", r=2)
        tmp256 = ar(TMP256, 256)
        bb = ar(BBW, 512).rearrange("p (r n) -> p r n", r=2)
        pw = ar(PWW, 288).rearrange("p (r a k) -> p r a k", r=2, a=PAIRS)
        pwr = ar(PWR, 256).rearrange("p (r a k) -> p r a k", r=2, a=PAIRS)
        small = {}
        at = PICK
        for name, w in (("vtop", 288), ("itop", 288), ("itf", 288), ("mark", 8), ("smx", 144), ("mx1", NTILE),
                        ("pos", 144), ("posab", 288), ("pf", 288), ("tick", 1), ("quad", 144)):
            small[name] = ar(at, w)
            at += w
        two = lambda v: v.rearrange("p (c t k) -> p c t k", c=2, t=NTILE)
        one = lambda v: v.rearrange("p (t k) -> p t k", t=NTILE)
        vtop, itf, pf, mark = two(small["vtop"]), two(small["itf"]), two(small["pf"]), small["mark"]
        itop, posab = two(small["itop"].bitcast(U32)), two(small["posab"].bitcast(U32))
        smx, mx1, pos, quad, tick = one(small["smx"]), one(small["mx1"]), one(small["pos"].bitcast(U32)), one(small["quad"].bitcast(U32)), small["tick"]

        def iall(a, n, t0, nt, h):
            v = ar(IALL + 1152 * a + P * t0, P * nt, n).rearrange("p (t j) -> p t j", t=nt)
            return v[:, :, bass.ds(TOPK * h, TOPK)]

        def itc(a, b, n, k):
            return ar(ITR + NT * a, NT)[:, bass.ds(64 * b + n, k)]

        S = {}

        def s(name):
            if name not in S:
                S[name] = sem(name)
            return S[name]

        plan, where = [], {}

        def jobs(stage, n, who):
            for i in range(n):
                where[stage, i] = len(plan)
                plan.append(who(i) if callable(who) else who)

        jobs("mod", 12, "dve")
        jobs("modT", 1, "act")
        jobs("g1", 4, "act")
        jobs("h1T", 24, lambda i: "act" if i % 2 else "dve")
        jobs("z", 24, lambda i: "dve" if i < 12 else "act")
        jobs("us", 9, "act")
        jobs("gate", 24, "act")
        jobs("k0", 8, "act")
        jobs("ug", 11, "act")
        jobs("rt", 8, "act")
        jobs("v", 16, "dve")
        jobs("y", 16, "act")
        jobs("gyT", 12, "dve")
        jobs("glu", 12, "act")
        jobs("rms", 1, "dve")
        jobs("mix", 36, "dve")
        jobs("h2T", 24, lambda i: "act" if i % 2 else "dve")
        n_stage = {}
        for (stage, i) in where:
            n_stage[stage] = max(n_stage.get(stage, 0), i + 1)
        emptied = {"act": s("banks_emptied_by_act"), "dve": s("banks_emptied_by_dve")}
        bank_full = s("bank_full")

        def empties(upto, e):
            return sum(p == e for p in plan[:upto])

        def bank_for(pe, stage, i):
            j = where[stage, i]
            if j >= 8:
                pe.wait_ge(emptied[plan[j - 8]], empties(j - 7, plan[j - 8]))
            return ps[j % 8]

        def filled(eng, stage, i):
            j = where[stage, i]
            eng.wait_ge(bank_full, j + 1)
            return ps[j % 8]

        def stage_emptied(eng, stage, n=None):
            upto = where[stage, (n or n_stage[stage]) - 1] + 1
            for e in ("act", "dve"):
                if empties(upto, e):
                    eng.wait_ge(emptied[e], empties(upto, e))

        block = ctx.enter_context(nc.Block())

        def group(q, e):
            return 8 * (q // 2) + 2 * e + q % 2

        def cols(t):
            return (t * P, P) if t < 8 else (SEQ, DSEQ)

        def modulated(eng, who, stage, dst, sc, sh):
            for j in range(8):
                for q in range(3):
                    if plan[where[stage, 3 * j + q]] != who:
                        continue
                    b = filled(eng, stage, 3 * j + q)
                    width, g = (512, 0) if q < 2 else (DSEQ, 1)
                    at = NT * j + 512 * q
                    out = dst[:, at:at + width] if dst is h2_buf else ar(dst + at, width)
                    if who == "act":
                        nc.scalar.activation(out, b[:, 0:width], ACT.Identity, bias=mcol[:, sh + j, g:g + 1],
                                scale=sc[:, j, g:g + 1]).then_inc(emptied["act"], 1)
                    else:
                        nc.vector.tensor_scalar(out, b[:, 0:width], sc[:, j, g:g + 1], mcol[:, sh + j, g:g + 1],
                                                ALU.mult, ALU.add).then_inc(emptied["dve"], 1)

        @block.sync
        def _(sp):
            def load(dst, src, name, n=16):
                sp.dma_start(dst, src).then_inc(s(name), n)

            load(prm[:, :], A["pack"], "params_in")
            load(ar(BROW, 6144, 2), A["b_ada"], "b_ada_in")
            load(ddg, A["ddiag"], "params_in")
            wv = A["w_ada"].rearrange("(k p) n -> p k n", p=P)
            for n in range(12):
                if n >= 2:
                    sp.wait_ge(bank_full, where["mod", n - 2] + 1)
                load(ar(WADA + 4096 * (n % 2), 4096).rearrange("p (k n) -> p k n", k=8),
                     wv[:, :, 512 * n:512 * n + 512], f"w_ada_in{n % 2}")
                if n == 3:
                    load(ar(X0, 8192).rearrange("p (k d) -> p k d", k=8), A["xp"], "x_in")
                    load(ar(X0 + 8192, 1024, DSEQ), A["xs"], "x_in")
                if n == 5:
                    load(ar(WIN, 12288).rearrange("p (k n) -> p k n", k=8),
                         A["w_in"].rearrange("(k p) n -> p k n", p=P), "w_in_in")
            with nc.allow_non_contiguous_dma(reason="last rows of a channel-major buffer"):
                stage_emptied(sp, "z", 12)
                for m in range(ML):
                    sp.dma_start(O["conv_p"][:, m, :], ar(XAP + 1027 * m + 1024, 3)).then_inc(s("states_out"), 16)
                    sp.dma_start(O["conv_s"][:, m, :], ar(XAS + 67 * m + 64, 3)).then_inc(s("states_out"), 16)
            stage_emptied(sp, "us")
            for k in range(L):
                load(ar(U8_, 4096, NCS).rearrange("p (g k i) -> p k g i", g=G, k=L)[:, k],
                     ar(US_, 512)[8 * k:8 * k + 8, :].rearrange("p (g i) -> p g i", g=G), "u8_in")
            sp.wait_ge(s("k0_ready"), 1)
            sp.wait_ge(s("t_zeroed"), 1)
            tv = ar(TT, 4096).rearrange("p (g n) -> p g n", g=G)
            kv = ar(K0, 4096, GS).rearrange("p (g n) -> p g n", g=G)
            for j in range(L):
                load(tv[GS * j:GS * j + GS, :, GS * j:P], kv[:, :, 0:P - GS * j], "toeplitz_in")
            stage_emptied(sp, "y")
            for k in range(L):
                load(ar(YS_, 512)[8 * k:8 * k + 8, :], ar(Y8_ + 512 * k, 512, NCS), "ys_in")
            sp.wait_ge(s("fin_ready"), 2)
            sp.dma_start(O["fin"], fin[:, :]).then_inc(s("states_out"), 16)
            load(ar(WGLU, 2048).rearrange("p (k n) -> p k n", k=4), A["w_glu"].rearrange("(k p) n -> p k n", p=P),
                 "w_glu_in")
            load(ar(WOUT, 8192).rearrange("p (k n) -> p k n", k=8), A["w_out"].rearrange("(k p) n -> p k n", p=P),
                 "w_out_in")
            load(ar(X1, 8192).rearrange("p (k d) -> p k d", k=8), A["xp"], "x_again_in")
            load(ar(X1 + 8192, 1024, DSEQ), A["xs"], "x_again_in")
            sp.wait_ge(s("x1_ready"), NTILE)
            sp.dma_start(x1d[:, 0:8192], ar(X1, 8192)).then_inc(s("x1_out"), 16)
            sp.dma_start(x1d[0:DSEQ, 8192:9216], ar(X1 + 8192, 1024, DSEQ)).then_inc(s("x1_out"), 16)
            sp.wait_ge(s("x1_out"), 32)
            stage_emptied(sp, "h2T")
            load(ar(KEYS, 2048), A["keys"], "keys_in")
            for h in range(2):
                load(seg(wq_buf, 2048 * h, 2048), A["wq"][h], f"wq_in{h}")
            with sp.Fori(0, HEADS // 2 - 1) as i:
                for h in range(2):
                    sp.wait_ge(s("s_full"), 4 * i + 2 * h + 2)
                    load(seg(wq_buf, 2048 * h, 2048), A["wq"][bass.ds(2 * i + (2 + h), 1)].rearrange("h p n -> (h p) n"),
                         f"wq_in{h}")

            def store_block(b, buf):
                sp.wait_ge(s("c_moved"), 16 * b + 16)
                sp.dma_start(coef[:, :, bass.ds(b, 1), :, :].rearrange("g p b e n -> p g (b e n)"),
                             ar(CB + 8192 * buf, 8192).rearrange("p (g n) -> p g n", g=64)).then_inc(
                    s(f"coef_out{buf}"), 16)

            sp.wait_ge(s("picksT_moved"), 9)
            for e in range(2):
                load(seg(u_in_buf, 1024 * e, 1024), A["ut"][e], f"u_in{e}")
            with sp.Fori(0, 8) as i:
                store_block(2 * i, 0)
                store_block(2 * i + 1, 1)
            store_block(16, 0)
            sp.wait_ge(s("coef_out0"), 16 * 9)
            sp.wait_ge(s("coef_out1"), 16 * 8)

            def load_experts(t, u, first, second=False):
                for e in range(0 if first else 2):
                    sp.wait_ge(s("s_bank_full"), 6 * t - 3 + 3 * e)
                    load(seg(u_in_buf, 1024 * e, 1024), A["ut"][bass.ds(2 * t + e, 1)].rearrange("t p n -> (t p) n"),
                         f"u_in{e}")
                if not first:
                    sp.wait_ge(s("w_weighed"), 6 * t)
                load(seg(c_in_buf, 0, 2176), coef[bass.ds(t, 1)].rearrange("t p b e n -> (t p) (b e n)"), "c_in")
                if not (first or second):
                    sp.wait_ge(s("v_bank_full"), 24 * (t - 1))
                load(seg(v_in_buf, 2048 * u, 2048), A["vt"][bass.ds(t, 1)].rearrange("t p n -> (t p) n"), f"v_in{u}")

            load_experts(0, 0, True)
            load_experts(1, 1, False, True)
            with sp.Fori(1, 32) as i:
                load_experts(2 * i, 0, False)
                load_experts(2 * i + 1, 1, False)
            sp.wait_ge(s("s_bank_full"), 6 * 64)
            load(seg(x1_buf, 0, 8192), x1d[:, 0:8192], "x1_back")
            load(seg(x1_buf, 8192, 1024, DSEQ), x1d[0:DSEQ, 8192:9216], "x1_back")
            load(seg(norm_f_buf, 0, 1024), A["norm_f"], "norm_f_in")
            for t in range(8):
                sp.wait_ge(s("y_ready"), t + 1)
                sp.dma_start(O["yp"][:, t, :], seg(x1_buf, 1024 * t, 1024)).then_inc(s("y_out"), 16)
            sp.wait_ge(s("y_ready"), 9)
            sp.dma_start(O["ys"], seg(x1_buf, 8192, 1024, DSEQ)).then_inc(s("y_out"), 16)
            sp.wait_ge(s("y_out"), 16 * 9)
            sp.wait_ge(s("states_out"), 16 * 9)

        @block.gpsimd
        def _(pool):
            nc.gpsimd.memset(ident[:, :], 0.0).then_inc(s("ident_zero"), 1)
            nc.gpsimd.memset(ones[:, :], 1.0).then_inc(s("const_ready"), 1)
            nc.gpsimd.iota(iota[:, :], [[1, P]], base=0, channel_multiplier=0,
                           allow_small_or_imprecise_dtypes=True).then_inc(s("const_ready"), 1)
            pool.wait_ge(s("ident_zero"), 1)
            nc.gpsimd.affine_select(out=ident[:, :], in_=ident[:, :], compare_op=ALU.not_equal, fill=1.0, base=0,
                                    pattern=[[-1, P]], channel_multiplier=1).then_inc(s("const_ready"), 1)
            pool.wait_ge(s("const_ready"), 3)
            for r in range(2):
                nc.gpsimd.tensor_copy(sel[:, r, :], ident[0:2, r:r + 1].to_broadcast([2, P])).then_inc(
                    s("const_ready"), 1)

            def decode(h):
                cnt = [0]

                def lk(ins):
                    cnt[0] += 1
                    ins.then_inc(s("decode_chain"), 1)
                    pool.wait_ge(s("decode_chain"), 11 * h + cnt[0])

                pool.wait_ge(s("positions_ready"), h + 1)
                for c in range(2):
                    sides = []
                    for n, t0, nt in ((P, 0, 8), (DSEQ, 8, 1)):
                        flat = ar((D0, D1)[c] + 256 * t0, 256 * nt, n)
                        sides.append((n, t0, nt, flat.rearrange("p (t j a) -> p t j a", t=nt, j=TOPK),
                                      [n, nt, TOPK, TOPK]))
                    if c == 1:
                        for n, t0, nt, v4, shp in sides:
                            last = nc.gpsimd.tensor_tensor(
                                v4, pf[0:n, c, t0:t0 + nt, :].unsqueeze(3).to_broadcast(shp),
                                iota[0:n, 0:TOPK].unsqueeze(1).unsqueeze(1).to_broadcast(shp), ALU.subtract)
                        lk(last)
                        nc.gpsimd.tensor_tensor(tick[:, :], iota[:, 0:1], iota[:, 0:1], ALU.add)
                        for n, t0, nt, v4, shp in sides:
                            flat = ar(D1 + 256 * t0, 256 * nt, n)
                            last = nc.gpsimd.tensor_scalar(flat, flat, 0.0, None, ALU.is_equal)
                        lk(last)
                    for n, t0, nt, v4, shp in sides:
                        last = nc.gpsimd.tensor_tensor(
                            v4, v4, itf[0:n, c, t0:t0 + nt, :].unsqueeze(2).to_broadcast(shp), ALU.mult)
                    lk(last)
                    for half in (8, 4, 2, 1):
                        for n, t0, nt, v4, shp in sides:
                            out = v4[:, :, :, 0:half] if half > 1 else iall(c, n, t0, nt, h).unsqueeze(3)
                            last = nc.gpsimd.tensor_tensor(out, v4[:, :, :, 0:half], v4[:, :, :, half:2 * half],
                                                           ALU.add)
                        if half > 1 or c == 0:
                            lk(last)
                last.then_inc(s("decoded"), 1)
                pool.wait_ge(s("decoded"), h + 1)
                assert cnt[0] == 11

            with pool.Fori(0, HEADS - 1) as h:
                decode(h)

            def gate_rows(b):
                for g in range(8):
                    pool.wait_ge(s("onehots_ready"), 8 * b + g + 1)
                    rows = ar(PQ + 2048 * (g % 4) + 1024, 1024).rearrange("p (j n) -> p j n", j=8)
                    nc.gpsimd.tensor_tensor(rows, rows, itc(2, b, 8 * g, 8).unsqueeze(2).to_broadcast([P, 8, P]),
                                            ALU.mult).then_inc(s("rows_ready"), 1)

            def u_rest(t):
                for e in range(2):
                    o = 1024 * e
                    pool.wait_ge(s(f"u_hi_ready{e}"), t + 1)
                    nc.gpsimd.tensor_tensor(u_lo[:, o:o + 1024], seg(u_in_buf, o, 1024), u_hi[:, o:o + 1024].bitcast(F32),
                                            ALU.subtract).then_inc(s(f"u_lo_ready{e}"), 1)

            pool.wait_ge(s("picksT_moved"), 9)
            gate_rows(0)
            u_rest(0)
            gate_rows(1)
            with pool.Fori(1, 8) as i:
                gate_rows(2 * i)
                gate_rows(2 * i + 1)
            gate_rows(16)

            def v_rest(u, i):
                o = 2048 * u
                pool.wait_ge(s(f"v_hi_ready{u}"), i + 1)
                nc.gpsimd.tensor_tensor(v_lo[:, o:o + 2048], seg(v_in_buf, o, 2048), v_hi[:, o:o + 2048].bitcast(F32),
                                        ALU.subtract).then_inc(s(f"v_lo_ready{u}"), 1)

            with pool.Fori(0, 31) as i:
                for u in range(2):
                    u_rest(2 * i + (1 + u))
                    v_rest(u, i)
            u_rest(63)
            v_rest(0, 31)
            v_rest(1, 31)

        @block.tensor
        def _(pe):
            mm = nc.tensor.matmul
            full = lambda ins: ins.then_inc(bank_full, 1)
            pe.wait_ge(s("csil_ready"), 1)
            cs = csil[:, :].rearrange("p (k s) -> p k s", s=2)
            for n in range(12):
                pe.wait_ge(s(f"w_ada_in{n % 2}"), 16 * (n // 2 + 1))
                b = bank_for(pe, "mod", n)
                w = ar(WADA + 4096 * (n % 2), 4096).rearrange("p (k n) -> p k n", k=8)
                for k in range(8):
                    last = mm(b[0:2, :], cs[:, k, :], w[:, k, :], start=k == 0, stop=k == 7)
                full(last)
            pe.wait_ge(s("const_ready"), 5)
            stage_emptied(pe, "mod")
            b = bank_for(pe, "modT", 0)
            for j in range(48):
                last = mm(b[:, 2 * j:2 * j + 2], ar(MROW + P * j, P, 2), ident[0:2, 0:2], start=True, stop=True)
            full(last)
            for q in range(4):
                b = bank_for(pe, "g1", q)
                full(mm(b[:, :], sel[:, q // 2, :],
                        ar(MROW + 2048 + 512 * (q % 2), 512, 2), start=True, stop=True))

            def turn(stage, nd, src, srcs):
                for j in range(nd):
                    for q in range(3):
                        b = bank_for(pe, stage, 3 * j + q)
                        if q < 2:
                            for t in range(4):
                                last = nc.tensor.transpose(b[:, P * t:P * t + P], src(4 * q + t, j), ident[:, :])
                        else:
                            last = nc.tensor.transpose(b[:, 0:DSEQ], srcs(j), ident[0:DSEQ, 0:DSEQ])
                        full(last)

            pe.wait_ge(s("xn_ready"), NTILE)
            turn("h1T", 8, lambda t, j: ar(XN + 1024 * t + P * j, P), lambda j: ar(XN + 8192 + P * j, P, DSEQ))
            stage_emptied(pe, "h1T")
            pe.wait_ge(s("w_in_in"), 16)
            w = ar(WIN, 12288).rearrange("p (k n) -> p k n", k=8)
            h = ar(HT, 8704).rearrange("p (k n) -> p k n", k=8)
            for m in range(8):
                for q, (k0, nk, width) in enumerate(CHUNKS):
                    b = bank_for(pe, "z", 3 * m + q)
                    for k in range(8):
                        last = mm(b[:, 0:width], w[:, k, P * m:P * m + P], h[:, k, P * k0:P * k0 + width],
                                  start=k == 0, stop=k == 7)
                    full(last)
            for t in range(NTILE):
                b = bank_for(pe, "us", t)
                c0, n = cols(t)
                for k in range(8):
                    last = mm(b[0:n, :], h[:, k, c0:c0 + n], w[:, k, 1024:1536], start=k == 0, stop=k == 7)
                full(last)
            for m in range(ML):
                pe.wait_ge(s("xc_ready"), 2 * (m + 1))
                for gate, name in enumerate(("wa", "wx")):
                    for q in range(3):
                        b = bank_for(pe, "gate", 6 * m + 3 * gate + q)
                        width = CHUNKS[q][2]
                        full(mm(b[:, 0:width], par(name)[:, P * m:P * m + P],
                                ar(XC + NT * m + 384 * q, width), start=True, stop=True))
            pe.wait_ge(s("oc_ready1"), 1)
            oc = [ar(OC + 2304 * r, 2304).rearrange("p (a n) -> p a n", a=PAIRS) for r in range(2)]
            for q in range(8):
                b = bank_for(pe, "k0", q)
                for e in range(4):
                    g = group(q, e)
                    lo, pair = 64 * (g % 2), g // 2
                    for r in range(2):
                        last = mm(b[0:GS, P * e:P * e + P],
                                  bb[lo:lo + 64, r, GS * pair:GS * pair + GS], oc[r][lo:lo + 64, pair, 0:P],
                                  start=r == 0, stop=r == 1)
                full(last)
            stage_emptied(pe, "us")
            pe.wait_ge(s("u8_in"), 16 * L)
            uv = ar(UT_, 4096).rearrange("p (g n) -> p g n", g=G)
            u8 = ar(U8_, 4096, NCS).rearrange("p (g n) -> p g n", g=G)
            for q in range(11):
                b = bank_for(pe, "ug", q)
                for n, g in enumerate(range(3 * q, min(3 * q + 3, G))):
                    nc.tensor.transpose(b[:, 136 * n:136 * n + P], uv[:, g], ident[:, :])
                    last = nc.tensor.transpose(b[:, 136 * n + P:136 * n + 136], u8[:, g], ident[0:NCS, 0:NCS])
                full(last)
            pe.wait_ge(s("xr_ready"), 1)
            for q in range(8):
                b = bank_for(pe, "rt", q)
                for n in range(4):
                    pair, r = (4 * q + n) // 2, n % 2
                    last = nc.tensor.transpose(b[:, P * n:P * n + P], ar(XR + 2048 * r + P * pair, P), ident[:, :])
                full(last)
            stage_emptied(pe, "rt")
            rt = ar(RT, 4096).rearrange("p (a r n) -> p a r n", a=PAIRS, r=2)
            ug = ar(UG, 4352).rearrange("p (g n) -> p g n", g=G)
            for a in range(PAIRS):
                b = bank_for(pe, "v", a)
                for e in range(2):
                    for r in range(2):
                        last = mm(b[64 * e:64 * e + 64, 136 * r:136 * r + 136], rt[:, a, r, 64 * e:64 * e + 64],
                                  ug[:, 2 * a + e, :], start=True, stop=True)
                full(last)
            pe.wait_ge(s("toeplitz_in"), 16 * L)
            pe.wait_ge(s("state_ready"), 1)
            tt = ar(TT, 4096).rearrange("p (g n) -> p g n", g=G)
            st = [ar(VV + SFLAT * r, SFLAT).rearrange("p (a n) -> p a n", a=PAIRS) for r in range(2)]
            for q in range(16):
                b = bank_for(pe, "y", q)
                u0, s0, n = ((0, 0, NC), (NC, NC + 1, NCS))[q // 8]
                for e in range(4):
                    g = group(q % 8, e)
                    lo, pair = 64 * (g % 2), g // 2
                    out = b[0:n, P * e:P * e + P]
                    mm(out, ug[:, g, u0:u0 + n], tt[:, g, :], start=True, stop=False)
                    for r in range(2):
                        last = mm(out, st[r][lo:lo + 64, pair, s0:s0 + n], oc[r][lo:lo + 64, pair, GS:GS + P],
                                  start=False, stop=r == 1)
                full(last)
            stage_emptied(pe, "y")
            pe.wait_ge(s("ys_in"), 16 * L)
            turn("gyT", 4, lambda t, j: ar(YT_ + 512 * t + P * j, P), lambda j: ar(YS_ + P * j, P, DSEQ))
            stage_emptied(pe, "gyT")
            pe.wait_ge(s("w_glu_in"), 16)
            w = ar(WGLU, 2048).rearrange("p (k n) -> p k n", k=4)
            for m in range(ML):
                for q, (k0, nk, width) in enumerate(CHUNKS):
                    b = bank_for(pe, "glu", 3 * m + q)
                    for k in range(4):
                        last = mm(b[:, 0:width], w[:, k, P * m:P * m + P], ar(GYT + NT * k + P * k0, width),
                                  start=k == 0, stop=k == 3)
                    full(last)
            b = bank_for(pe, "rms", 0)
            for half in range(2):
                pe.wait_ge(s("sq_ready"), half + 1)
                for t in range(NTILE):
                    c0, n = cols(t)
                    for k in range(4):
                        last = mm(b[0:n, 9 * half + t:9 * half + t + 1], ar(SQ + 4352 * half + NT * k + c0, n),
                                  ones[:, :], start=k == 0, stop=k == 3)
            full(last)
            pe.wait_ge(s("halves_scaled"), 2)
            pe.wait_ge(s("w_out_in"), 16)
            w = ar(WOUT, 8192).rearrange("p (k n) -> p k n", k=8)
            for t in range(NTILE):
                c0, n = cols(t)
                for nh in range(2):
                    for half, src in enumerate((YL, YS5)):
                        b = bank_for(pe, "mix", 4 * t + 2 * nh + half)
                        for k in range(4):
                            last = mm(b[0:n, :], ar(src + NT * k + c0, n), w[:, 4 * half + k, 512 * nh:512 * nh + 512],
                                      start=k == 0, stop=k == 3)
                        full(last)
            pe.wait_ge(s("xn2_ready"), NTILE)
            turn("h2T", 8, lambda t, j: ar(XN2 + 1024 * t + P * j, P), lambda j: ar(XN2 + 8192 + P * j, P, DSEQ))
            stage_emptied(pe, "h2T")

            h2 = seg(h2_buf, 0, 8704).rearrange("p (k n) -> p k n", k=8)
            pe.wait_ge(s("keys_in"), 16)

            def head(hd, hb, i, first=False):
                pe.wait_ge(s("kbuf_ready"), hd + 1)
                pe.wait_ge(s(f"wq_in{hb}"), 16 * i + 16)
                for c in range(2):
                    w = seg(wq_buf, 2048 * hb + 1024 * c, 1024).rearrange("p (k n) -> p k n", k=8)
                    for q, (k0, nk, width) in enumerate(CHUNKS):
                        for k in range(8):
                            last = mm(ps[q][:, 0:width], w[:, k, :], h2[:, k, P * k0:P * k0 + width],
                                      start=k == 0, stop=k == 7)
                    last.then_inc(s("q_full"), 1)
                    pe.wait_ge(s("q_moved"), 2 * hd + c + 1)
                    if not (first and c == 0):
                        pe.wait_ge(s("s_moved"), 2 * hd + c)
                    for t in range(NTILE):
                        c0, n = cols(t)
                        last = mm(ps[3 + t // 4][0:n, P * (t % 4):P * (t % 4) + P], ar(QT + NT * c + c0, n),
                                  kbuf[:, c, :], start=True, stop=True)
                    last.then_inc(s("s_full"), 1)

            kbuf = ar(WK, 256).rearrange("p (c n) -> p c n", c=2)

            head(0, 0, 0, True)
            head(1, 1, 0)
            with pe.Fori(1, HEADS // 2) as i:
                head(2 * i, 0, i)
                head(2 * i + 1, 1, i)

            pe.wait_ge(s("picks_ready"), HEADS)
            pe.wait_ge(s("decoded"), HEADS - 1)
            for a in range(3):
                for q in range(3):
                    if 3 * a + q == 8:
                        pe.wait_ge(s("picksT_moved"), 1)
                    for t in range(4 * q, min(4 * q + 4, NTILE)):
                        c0, n = cols(t)
                        last = nc.tensor.transpose(ps[(3 * a + q) % 8][:, P * (t % 4):P * (t % 4) + n],
                                                   ar(IALL + 1152 * a + P * t, P, n), ident[0:n, 0:n])
                    last.then_inc(s("picksT_full"), 1)

            pe.wait_ge(s("picksT_moved"), 9)

            def coef_block(b, first):
                for g in range(8):
                    pe.wait_ge(s("rows_ready"), 8 * b + g + 1)
                    if not (first and g < 4):
                        pe.wait_ge(s("c_moved"), 16 * b + 2 * g - 6)
                    for j in range(8):
                        bank = ps[2 * (g % 4) + j // 4]
                        last = mm(bank[:, P * (j % 4):P * (j % 4) + P], ar(PQ + 2048 * (g % 4) + P * j, P),
                                  ar(PQ + 2048 * (g % 4) + 1024 + P * j, P), start=True, stop=True)
                    last.then_inc(s("c_full"), 1)

            coef_block(0, True)
            coef_block(1, False)
            with pe.Fori(1, 8) as i:
                coef_block(2 * i, False)
                coef_block(2 * i + 1, False)
            coef_block(16, False)
            pe.wait_ge(s("c_moved"), 16 * 17)

            parts = ((0, 0), (0, 1), (1, 0))

            def scores(t, u, first=False):
                ph = [v[:, :].rearrange("p (k n) -> p k n", k=8) for v in (h_hi, h_lo)]
                for e in range(2):
                    w = [v[:, 1024 * e:1024 * e + 1024].rearrange("p (k n) -> p k n", k=8) for v in (u_hi, u_lo)]
                    pe.wait_ge(s(f"u_lo_ready{e}"), t + 1)
                    for q, (k0, nk, width) in enumerate(CHUNKS):
                        j = 3 * e + q
                        if not (first and j < 4):
                            pe.wait_ge(s("s_gelu"), 6 * t + j - 3)
                        for k in range(8):
                            for n, (a, b) in enumerate(parts):
                                last = mm(ps[(6 * u + j) % 4][:, 0:width], w[a][:, k, :],
                                          ph[b][:, k, P * k0:P * k0 + width], start=k == 0 and n == 0,
                                          stop=k == 7 and n == 2)
                        last.then_inc(s("s_bank_full"), 1)

            def values(t, u, i, first=False):
                pe.wait_ge(s(f"v_lo_ready{u}"), i + 1)
                pe.wait_ge(s("w_lo_ready"), 6 * t + 6)
                for d in range(8):
                    for q, (k0, nk, width) in enumerate(CHUNKS):
                        j = 3 * d + q
                        if not (first and j < 4):
                            pe.wait_ge(s("y_added"), 24 * t + j - 3)
                        for e in range(2):
                            for n, (a, b) in enumerate(parts):
                                o, ow = 2048 * u + 1024 * e + P * d, 2176 * u + NT * e + P * k0
                                last = mm(ps[4 + j % 4][:, 0:width], (v_hi, v_lo)[a][:, o:o + P],
                                          (w_hi, w_lo)[b][:, ow:ow + width], start=e == 0 and n == 0,
                                          stop=e == 1 and n == 2)
                        last.then_inc(s("v_bank_full"), 1)

            pe.wait_ge(s("h_split"), 2)
            scores(0, 0, True)
            scores(1, 1)
            values(0, 0, 0, True)
            with pe.Fori(1, 32) as i:
                scores(2 * i, 0)
                values(2 * i - 1, 1, i - 1)
                scores(2 * i + 1, 1)
                values(2 * i, 0, i)
            values(63, 1, 31)
            for t in range(NTILE):
                c0, n = cols(t)
                if t == 0:
                    pe.wait_ge(s("y_scaled"), 1)
                if t >= 4:
                    pe.wait_ge(s("x2_done"), t - 3)
                for d in range(8):
                    last = nc.tensor.transpose(ps[2 * (t % 4) + d // 4][0:n, P * (d % 4):P * (d % 4) + P],
                                               seg(y_sum_buf, NT * d + c0, n), ident[:, :])
                last.then_inc(s("yT_full"), 1)

        @block.scalar
        def _(act):
            av = nc.scalar.activation
            done = lambda ins: ins.then_inc(emptied["act"], 1)
            act.wait_ge(s("params_in"), 32)
            av(csil[:, :], par("cT"), ACT.Sigmoid).then_inc(s("csig_ready"), 1)
            av(s5c[:, 0, :], par("ldt"), ACT.Exp).then_inc(s("s5_dt_ready"), 1)
            act.wait_ge(s("s5_lrdt_ready"), 1)
            av(s5c[:, 3, :], s5c[:, 1, :], ACT.Exp).then_inc(s("s5_mag_ready"), 1)
            av(s5c[:, 4, :], s5c[:, 1, :], ACT.Exp, scale=float(L)).then_inc(s("s5_mag_ready"), 1)
            act.wait_ge(s("lam_abs_ready"), 1)
            av(lrc[:, 4:8], lrc[:, 0:4], ACT.Exp, scale=-1.0).then_inc(s("lam_exp_ready"), 1)
            act.wait_ge(s("lam_w_ready"), 1)
            av(lrc[:, 12:16], lrc[:, 8:12], ACT.Ln).then_inc(s("lam_ln_ready"), 1)
            for f in range(2):
                act.wait_ge(s("phase_ready"), f + 1)
                av(s5c[:, 8 + 4 * f, :], s5c[:, 7 + 4 * f, :], ACT.Sin).then_inc(s("sin_ready"), 1)
                av(s5c[:, 9 + 4 * f, :], s5c[:, 7 + 4 * f, :], ACT.Sin, scale=0.5).then_inc(s("sin_ready"), 1)
            b = filled(act, "modT", 0)
            done(nc.scalar.copy(mcol[:, :, :].rearrange("p j s -> p (j s)"), b[:, 0:96]))
            for q in range(4):
                b = filled(act, "g1", q)
                done(nc.scalar.copy(ar(G1B + 512 * q, 512), b[:, :]))
            act.wait_ge(s("x_in"), 32)
            for t in range(NTILE):
                n = cols(t)[1]
                if t:
                    act.wait_ge(s("ssq1"), t)
                av(ar(JUNK0, 1024, n), ar(X0 + 1024 * t, 1024, n), ACT.Square, accum_out=ssq[0:n, t:t + 1]).then_inc(
                    s("ssq1"), 1)
            act.wait_ge(s("ms1_ready"), 2)
            av(ssq[:, 18:26], ssq[:, 9:17], ACT.Sqrt).then_inc(s("rt1_ready"), 1)
            av(ssq[0:DSEQ, 26:27], ssq[0:DSEQ, 17:18], ACT.Sqrt).then_inc(s("rt1_ready"), 1)

            act.wait_ge(s("a1_ready"), 1)
            stage_emptied(act, "g1")
            modulated(act, "act", "h1T", HT, a1, 0)
            for m in range(4):
                for q, (k0, nk, width) in enumerate(CHUNKS):
                    b = filled(act, "z", 12 + 3 * m + q)
                    out = ar(GA + NT * m, SEQ).rearrange("p (c k) -> p k c", k=L)[:, k0:k0 + nk, :]
                    last = av(out, b[:, 0:P * nk].rearrange("p (k c) -> p k c", k=nk), ACT.Gelu_apprx_tanh)
                    if q == 2:
                        out = ar(GA + NT * m + SEQ, DSEQ).rearrange("p (c k) -> p k c", k=L)
                        last = av(out, b[:, 256:320].rearrange("p (k c) -> p k c", k=L), ACT.Gelu_apprx_tanh)
                    done(last)
            for t in range(NTILE):
                b = filled(act, "us", t)
                n = cols(t)[1]
                if t < 8:
                    done(nc.scalar.copy(ar(UT_, 4096).rearrange("p (g k i) -> p k g i", g=G, k=L)[:, t],
                                        b[:, :].rearrange("p (g i) -> p g i", g=G)))
                else:
                    done(nc.scalar.copy(ar(US_, 512, n), b[0:n, :]))
            for m in range(ML):
                for gate, (dst, bias) in enumerate(((RG, "ba"), (IG, "bx"))):
                    for q in range(3):
                        b = filled(act, "gate", 6 * m + 3 * gate + q)
                        width = CHUNKS[q][2]
                        last = av(ar(dst + NT * m + 384 * q, width), b[:, 0:width], ACT.Sigmoid,
                                  bias=par(bias)[:, m:m + 1])
                        done(last)
            act.wait_ge(s("lam_ready"), 1)
            act.wait_ge(emptied["act"], empties(where["gate", 23] + 1, "act"))
            for m in range(ML):
                av(ar(TG + NT * m, NT), ar(RG + NT * m, NT), ACT.Tanh, scale=lrc[:, 20 + m:21 + m]).then_inc(
                    s("tanh_ready"), 1)
            act.wait_ge(s("tanh_ready"), 4)
            for m in range(ML):
                av(ar(RG + NT * m, NT), ar(RG + NT * m, NT), ACT.Exp, scale=lrc[:, 16 + m:17 + m]).then_inc(
                    s("decay_ready"), 1)
            act.wait_ge(s("ratio_ready"), 1)
            av(ar(TG, 4352), ar(TG, 4352), ACT.Sqrt, scale=2.0).then_inc(s("root_ready"), 1)
            act.wait_ge(s("input_ready"), 1)
            for q in range(8):
                b = filled(act, "k0", q)
                k0 = group(q, 0)
                done(nc.scalar.copy(ar(K0, 4096, GS).rearrange("p (g n) -> p g n", g=G)[:, k0:k0 + 7:2, :],
                                    b[0:GS, :].rearrange("p (g n) -> p g n", g=4)))
            act.wait_ge(s("yl_ready"), 1)
            for q in range(11):
                b = filled(act, "ug", q)
                n = 136 * (min(3 * q + 3, G) - 3 * q)
                done(nc.scalar.copy(ar(UG + 408 * q, n), b[:, 0:n]))
            for q in range(8):
                b = filled(act, "rt", q)
                done(nc.scalar.copy(ar(RT + 512 * q, 512), b[:, :]))
            for q in range(16):
                b = filled(act, "y", q)
                base, n = ((YT_, NC), (Y8_, NCS))[q // 8]
                out = ar(base, 4096, n).rearrange("p (k g i) -> p k g i", k=L, g=G)
                for e in range(4):
                    last = av(out[:, :, group(q % 8, e), :], b[0:n, P * e:P * e + P].rearrange("p (k i) -> p k i", k=L),
                              ACT.Gelu_apprx_tanh)
                done(last)
            for m in range(ML):
                for q, (k0, nk, width) in enumerate(CHUNKS):
                    b = filled(act, "glu", 3 * m + q)
                    done(av(ar(YS5 + NT * m + P * k0, width), b[:, 0:width], ACT.Sigmoid, bias=par("bglu")[:, m:m + 1]))
            act.wait_ge(s("yl_ready"), 1)
            stage_emptied(act, "gyT")
            av(ar(SQ, 4352), ar(YL, 4352), ACT.Square).then_inc(s("sq_ready"), 1)
            act.wait_ge(s("ys5_ready"), 1)
            av(ar(SQ + 4352, 4352), ar(YS5, 4352), ACT.Square).then_inc(s("sq_ready"), 1)
            act.wait_ge(s("ms2_ready"), 2)
            av(ssq[:, 0:16], ssq[:, 18:34], ACT.Sqrt).then_inc(s("rt2_ready"), 1)
            av(ssq[0:DSEQ, 16:18], ssq[0:DSEQ, 34:36], ACT.Sqrt).then_inc(s("rt2_ready"), 1)
            for t in range(NTILE):
                n = cols(t)[1]
                act.wait_ge(s("x1_ready"), t + 1)
                if t:
                    act.wait_ge(s("ssq3"), t)
                else:
                    act.wait_ge(s("ssq1"), NTILE)
                av(ar(JUNK3, 1024, n), ar(X1 + 1024 * t, 1024, n), ACT.Square, accum_out=rms3[0:n, t:t + 1]).then_inc(
                    s("ssq3"), 1)
            act.wait_ge(s("ms3_ready"), 2)
            av(rms3[:, 20:28], rms3[:, 10:18], ACT.Sqrt).then_inc(s("rt3_ready"), 1)
            av(rms3[0:DSEQ, 28:29], rms3[0:DSEQ, 18:19], ACT.Sqrt).then_inc(s("rt3_ready"), 1)
            act.wait_ge(s("a2_ready"), 1)
            modulated(act, "act", "h2T", h2_buf, a2, 24)

            act.wait_ge(s("keys_in"), 16)

            def head_moves(h, first):
                if not first:
                    act.wait_ge(s("s_full"), 2 * h)
                nc.scalar.copy(ar(WK, 256), ar(KEYS, 2048)[:, bass.ds(256 * h, 256)]).then_inc(s("kbuf_ready"), 1)
                for c in range(2):
                    act.wait_ge(s("q_full"), 2 * h + c + 1)
                    for q in range(3):
                        width = CHUNKS[q][2]
                        last = nc.scalar.copy(ar(QT + NT * c + 384 * q, width), ps[q][:, 0:width])
                    last.then_inc(s("q_moved"), 1)
                    act.wait_ge(s("s_full"), 2 * h + c + 1)
                    if not first:
                        act.wait_ge(s("scores_read"), 2 * h + c - 1)
                    for half in range(2):
                        nc.scalar.copy(ar(SB + 1152 * c + 512 * half, 512), ps[3 + half][:, :])
                    nc.scalar.copy(ar(SB + 1152 * c + 1024, P, DSEQ), ps[5][0:DSEQ, 0:P]).then_inc(s("s_moved"), 1)

            def softmax_exp(h):
                act.wait_ge(s("softmax_in"), h + 1)
                av(smx[:, 0:8, :], smx[:, 0:8, :], ACT.Exp)
                av(smx[0:DSEQ, 8, :], smx[0:DSEQ, 8, :], ACT.Exp).then_inc(s("softmax_exp"), 1)

            stage_emptied(act, "h2T")
            nc.scalar.copy(h_hi[:, :], seg(h2_buf, 0, 8704)).then_inc(s("h_split"), 1)
            head_moves(0, True)
            with act.Fori(1, HEADS) as h:
                head_moves(h, False)
                softmax_exp(h - 1)
            softmax_exp(HEADS - 1)

            for a in range(3):
                for q in range(3):
                    act.wait_ge(s("picksT_full"), 3 * a + q + 1)
                    width = (512, 512, DSEQ)[q]
                    nc.scalar.copy(ar(ITR + NT * a + 512 * q, width), ps[(3 * a + q) % 8][:, 0:width]).then_inc(
                        s("picksT_moved"), 1)


            def u_first(t):
                for e in range(2):
                    act.wait_ge(s(f"u_in{e}"), 16 * t + 16)
                    nc.scalar.copy(u_hi[:, 1024 * e:1024 * e + 1024], seg(u_in_buf, 1024 * e, 1024)).then_inc(
                        s(f"u_hi_ready{e}"), 1)

            def move_block(b, buf, first):
                if not first:
                    act.wait_ge(s(f"coef_out{buf}"), 8 * (b - buf))
                out = ar(CB + 8192 * buf, 8192).rearrange("p (i n) -> p n i", n=64)
                for g in range(8):
                    act.wait_ge(s("c_full"), 8 * b + g + 1)
                    for half in range(2):
                        n0 = 8 * g + 4 * half
                        nc.scalar.copy(out[:, n0:n0 + 4, :],
                                       ps[2 * (g % 4) + half][:, :].rearrange("p (n i) -> p n i", n=4)).then_inc(
                            s("c_moved"), 1)

            move_block(0, 0, True)
            u_first(0)
            move_block(1, 1, True)
            with act.Fori(1, 8) as i:
                move_block(2 * i, 0, False)
                move_block(2 * i + 1, 1, False)
            move_block(16, 0, False)

            def v_first(u, i):
                act.wait_ge(s(f"v_in{u}"), 16 * i + 16)
                nc.scalar.copy(v_hi[:, 2048 * u:2048 * u + 2048], seg(v_in_buf, 2048 * u, 2048)).then_inc(
                    s(f"v_hi_ready{u}"), 1)

            def gelus(t, u, first):
                if not first:
                    act.wait_ge(s("v_bank_full"), 24 * (t - 1))
                for j in range(7):
                    if j < 6:
                        k0, nk, width = CHUNKS[j % 3]
                        act.wait_ge(s("s_bank_full"), 6 * t + j + 1)
                        av(seg(w_in_buf, 2176 * u + NT * (j // 3) + P * k0, width), ps[(6 * u + j) % 4][:, 0:width],
                           ACT.Gelu_apprx_tanh).then_inc(s("s_gelu"), 1)
                    if j > 0:
                        k0, nk, width = CHUNKS[(j - 1) % 3]
                        o = 2176 * u + NT * ((j - 1) // 3) + P * k0
                        act.wait_ge(s("w_weighed"), 6 * t + j)
                        nc.scalar.copy(w_hi[:, o:o + width], seg(w_in_buf, o, width)).then_inc(s("w_hi_ready"), 1)

            act.wait_ge(s("coef_out0"), 16 * 9)
            act.wait_ge(s("coef_out1"), 16 * 8)
            gelus(0, 0, True)
            u_first(1)
            v_first(0, 0)
            gelus(1, 1, True)
            with act.Fori(1, 32) as i:
                u_first(2 * i)
                v_first(1, i - 1)
                gelus(2 * i, 0, False)
                u_first(2 * i + 1)
                v_first(0, i)
                gelus(2 * i + 1, 1, False)
            v_first(1, 31)
            for t in range(NTILE):
                n = cols(t)[1]
                act.wait_ge(s("x2_done"), t + 1)
                if t:
                    act.wait_ge(s("ssq4"), t)
                else:
                    act.wait_ge(s("ssq3"), NTILE)
                av(seg(square_buf, 0, 1024, n), seg(x1_buf, 1024 * t, 1024, n), ACT.Square, accum_out=rms4[0:n, t:t + 1]).then_inc(
                    s("ssq4"), 1)
            act.wait_ge(s("ms4_ready"), 2)
            av(rms4[:, 20:28], rms4[:, 10:18], ACT.Sqrt).then_inc(s("rt4_ready"), 1)
            av(rms4[0:DSEQ, 28:29], rms4[0:DSEQ, 18:19], ACT.Sqrt).then_inc(s("rt4_ready"), 1)

        @block.vector
        def _(dve):
            V = nc.vector
            chain = [0]

            def link(ins):
                chain[0] += 1
                ins.then_inc(s("dve_chain"), 1)
                dve.wait_ge(s("dve_chain"), chain[0])

            def tt(o, a, b, op):
                return V.tensor_tensor(o, a, b, op)

            def ts(o, a, x, y, op0, op1=None):
                return V.tensor_scalar(o, a, x, y, op0, op1) if op1 is not None else V.tensor_scalar(o, a, x, None, op0)

            done = lambda ins: ins.then_inc(emptied["dve"], 1)
            C = lambda i: s5c[:, i, :]
            dve.wait_ge(s("csig_ready"), 1)
            tt(csil[:, :], csil[:, :], par("cT"), ALU.mult).then_inc(s("csil_ready"), 1)
            dve.wait_ge(s("s5_dt_ready"), 1)
            tt(C(1), C(0), par("are"), ALU.mult).then_inc(s("s5_lrdt_ready"), 1)
            link(tt(C(2), C(0), par("aim"), ALU.mult))
            link(ts(lrc[:, 16:20], par("lam"), -1.0, None, ALU.mult))
            tt(lrc[:, 0:4], par("lam"), lrc[:, 16:20], ALU.max).then_inc(s("lam_abs_ready"), 1)
            dve.wait_ge(s("lam_exp_ready"), 1)
            ts(lrc[:, 8:12], lrc[:, 4:8], 1.0, None, ALU.add).then_inc(s("lam_w_ready"), 1)
            dve.wait_ge(s("lam_w_ready"), 1)
            link(ts(lrc[:, 20:24], lrc[:, 8:12], 1.0, None, ALU.is_equal))
            dve.wait_ge(s("lam_ln_ready"), 1)
            link(ts(lrc[:, 8:12], lrc[:, 8:12], -1.0, None, ALU.add))
            link(tt(lrc[:, 8:12], lrc[:, 8:12], lrc[:, 20:24], ALU.add))
            link(V.reciprocal(lrc[:, 8:12], lrc[:, 8:12]))
            link(tt(lrc[:, 12:16], lrc[:, 12:16], lrc[:, 20:24], ALU.add))
            link(tt(lrc[:, 12:16], lrc[:, 12:16], lrc[:, 4:8], ALU.mult))
            link(tt(lrc[:, 12:16], lrc[:, 12:16], lrc[:, 8:12], ALU.mult))
            link(ts(lrc[:, 16:20], lrc[:, 16:20], 0.0, None, ALU.max))
            link(tt(lrc[:, 12:16], lrc[:, 12:16], lrc[:, 16:20], ALU.add))
            link(ts(lrc[:, 20:24], lrc[:, 12:16], LRU_C, None, ALU.mult))
            ts(lrc[:, 16:20], lrc[:, 12:16], -LRU_C, None, ALU.mult).then_inc(s("lam_ready"), 1)
            for f in range(2):
                ph, t = C(7 + 4 * f), C(5)
                if f == 0:
                    link(V.tensor_copy(ph, C(2)))
                else:
                    link(ts(ph, C(7), float(L), None, ALU.mult))
                link(ts(t, ph, 1.0 / TWO_PI, MAGIC, ALU.mult, ALU.add))
                link(ts(t, t, -MAGIC, None, ALU.add))
                for part in (6.28125, 0.0019340515136718750, TWO_PI - 6.28125 - 0.0019340515136718750):
                    link(V.scalar_tensor_tensor(out=ph, in0=t, scalar=-part, in1=ph, op0=ALU.mult, op1=ALU.add))
                ts(ph, ph, 3.1415925, -3.1415925, ALU.min, ALU.max).then_inc(s("phase_ready"), 1)
                dve.wait_ge(s("phase_ready"), f + 1)
                dve.wait_ge(s("sin_ready"), 2 * f + 2)
                link(tt(C(10 + 4 * f), C(9 + 4 * f), C(9 + 4 * f), ALU.mult))
                link(ts(C(10 + 4 * f), C(10 + 4 * f), -2.0, 1.0, ALU.mult, ALU.add))
            dve.wait_ge(s("s5_mag_ready"), 2)
            tt(C(15), C(3), C(10), ALU.mult)
            link(tt(C(16), C(3), C(8), ALU.mult))
            lr, li = par("are"), par("aim")
            link(tt(C(17), lr, lr, ALU.mult))
            link(tt(C(18), li, li, ALU.mult))
            link(tt(C(17), C(17), C(18), ALU.add))
            link(V.reciprocal(C(17), C(17)))
            link(ts(C(18), C(15), -1.0, None, ALU.add))
            link(tt(C(19), C(18), lr, ALU.mult))
            link(tt(C(20), C(16), li, ALU.mult))
            link(tt(C(19), C(19), C(20), ALU.add))
            link(tt(C(20), C(16), lr, ALU.mult))
            link(tt(C(21), C(18), li, ALU.mult))
            link(tt(C(20), C(20), C(21), ALU.subtract))
            link(tt(C(19), C(19), C(17), ALU.mult))
            link(tt(C(20), C(20), C(17), ALU.mult))

            def b3(v, shape):
                return v.unsqueeze(2).to_broadcast(shape)

            def cmul(o_re, o_im, a_re, a_im, b_re, b_im, t1, neg=False, flag=None):
                tt(o_re, a_re, b_re, ALU.mult)
                link(tt(t1, a_im, b_im, ALU.mult))
                link(tt(o_re, o_re, t1, ALU.subtract))
                tt(o_im, a_im, b_re, ALU.mult)
                link(tt(t1, a_re, b_im, ALU.mult))
                if neg:
                    last = V.scalar_tensor_tensor(out=o_im, in0=o_im, scalar=-1.0, in1=t1, op0=ALU.mult,
                                                  op1=ALU.subtract)
                else:
                    last = tt(o_im, o_im, t1, ALU.add)
                if flag:
                    last.then_inc(s(flag), 1)
                    dve.wait_ge(s(flag), 1)
                else:
                    link(last)

            q3 = lambda v: v.rearrange("p (a i) -> p a i", a=PAIRS)
            sh = [P, PAIRS, GS]
            cmul(q3(bb[:, 0, :]), q3(bb[:, 1, :]), q3(par("bre")), q3(par("bim")), b3(C(19), sh), b3(C(20), sh),
                 q3(tmp256))
            link(V.memset(pw[:, 0, :, 0:1], 1.0))
            link(V.memset(pw[:, 1, :, 0:1], 0.0))
            link(V.tensor_copy(pw[:, 0, :, 1], C(15)))
            link(V.tensor_copy(pw[:, 1, :, 1], C(16)))
            for m in (1, 2, 4):
                shp = [P, PAIRS, m]
                cmul(pw[:, 0, :, m + 1:2 * m + 1], pw[:, 1, :, m + 1:2 * m + 1], pw[:, 0, :, 1:m + 1],
                     pw[:, 1, :, 1:m + 1], pw[:, 0, :, m:m + 1].to_broadcast(shp),
                     pw[:, 1, :, m:m + 1].to_broadcast(shp), tmp256[:, 0:PAIRS * m].rearrange("p (a m) -> p a m", m=m))
            for k in range(L):
                link(V.tensor_copy(pwr[:, :, :, k], pw[:, :, :, L - 1 - k]))

            for n in range(12):
                b = filled(dve, "mod", n)
                if n == 0:
                    dve.wait_ge(s("b_ada_in"), 16)
                done(tt(ar(MROW + 512 * n, 512, 2), b[0:2, :], ar(BROW + 512 * n, 512, 2), ALU.add))
            stage_emptied(dve, "modT")

            def one_plus(dst, sc0, norm, name):
                link(ts(dst[:, :, :], mcol[:, sc0:sc0 + 8, :], 1.0, None, ALU.add))
                tt(dst[:, :, :], dst[:, :, :], par(norm).unsqueeze(2).to_broadcast([P, 8, 2]), ALU.mult).then_inc(
                    s(name), 1)

            one_plus(a1, 8, "norm1", "a1_ready")
            one_plus(a2, 32, "norm2", "a2_ready")
            dve.wait_ge(s("ssq1"), NTILE)

            def rnorm(src, mid, root, n8, ns, width, ms, rt):
                ts(mid[:, 0:n8], src[:, 0:n8], 1.0 / width, EPS, ALU.mult, ALU.add).then_inc(s(ms), 1)
                ts(mid[0:DSEQ, n8:n8 + ns], src[0:DSEQ, n8:n8 + ns], 1.0 / width, EPS, ALU.mult, ALU.add).then_inc(
                    s(ms), 1)
                dve.wait_ge(s(rt), 2)
                link(V.reciprocal(root[:, 0:n8], root[:, 0:n8]))
                link(V.reciprocal(root[0:DSEQ, n8:n8 + ns], root[0:DSEQ, n8:n8 + ns]))

            rnorm(ssq[:, 0:9], ssq[:, 9:18], ssq[:, 18:27], 8, 1, DM, "ms1_ready", "rt1_ready")
            for t in range(NTILE):
                n = cols(t)[1]
                ts(ar(XN + 1024 * t, 1024, n), ar(X0 + 1024 * t, 1024, n), ssq[0:n, 18 + t:19 + t], None,
                   ALU.mult).then_inc(s("xn_ready"), 1)
            stage_emptied(dve, "g1")
            dve.wait_ge(s("a1_ready"), 1)
            modulated(dve, "dve", "h1T", HT, a1, 0)
            stage_emptied(dve, "h1T")
            for m in range(ML):
                link(V.memset(ar(XAP + 1027 * m, 3), 0.0))
                link(V.tensor_copy(ar(XAS + 67 * m, 3), par("cache")[:, 3 * m:3 * m + 3]))
            for m in range(ML):
                for q, (k0, nk, width) in enumerate(CHUNKS):
                    b = filled(dve, "z", 3 * m + q)
                    out = ar(XAP + 1027 * m + 3, SEQ).rearrange("p (c k) -> p k c", k=L)[:, k0:k0 + nk, :]
                    last = V.tensor_copy(out, b[:, 0:P * nk].rearrange("p (k c) -> p k c", k=nk))
                    if q == 2:
                        out = ar(XAS + 67 * m + 3, DSEQ).rearrange("p (c k) -> p k c", k=L)
                        last = V.tensor_copy(out, b[:, 256:320].rearrange("p (k c) -> p k c", k=L))
                    done(last)
            stage_emptied(dve, "z", 12)
            for m in range(ML):
                for dst, src, n in ((XC + NT * m, XAP + 1027 * m, SEQ), (XC + NT * m + SEQ, XAS + 67 * m, DSEQ)):
                    w = par("conv_w")
                    link(ts(ar(dst, n), ar(src + 3, n), w[:, 4 * m + 3:4 * m + 4], par("conv_b")[:, m:m + 1],
                            ALU.mult, ALU.add))
                    for k in range(3):
                        last = V.scalar_tensor_tensor(out=ar(dst, n), in0=ar(src + k, n),
                                                      scalar=w[:, 4 * m + k:4 * m + k + 1], in1=ar(dst, n),
                                                      op0=ALU.mult, op1=ALU.add)
                        if k < 2:
                            link(last)
                    last.then_inc(s("xc_ready"), 1)
            dve.wait_ge(s("states_out"), 16 * 8)
            sh4 = [P, PAIRS, 9, GS]
            f4 = lambda off, k: ar(off, PAIRS * k * GS).rearrange("p (a k i) -> p a k i", a=PAIRS, k=k)
            dup = lambda v, k: q3(v).unsqueeze(2).to_broadcast([P, PAIRS, k, GS])
            pb = lambda v, k: v.unsqueeze(3).to_broadcast([P, PAIRS, k, GS])
            for a in range(2):
                h8 = slice(8 * a, 8 * a + 8)
                cmul(f4(OC, 9)[:, h8], f4(OC + 2304, 9)[:, h8], dup(par("cre"), 9)[:, h8], dup(par("cim"), 9)[:, h8],
                     pb(pw[:, 0], 9)[:, h8], pb(pw[:, 1], 9)[:, h8],
                     ar(TMP1152, 1152).rearrange("p (a k i) -> p a k i", a=8, k=9), neg=True,
                     flag=f"oc_ready{a}")
            dve.wait_ge(bank_full, where["us", 8] + 1)
            cmul(f4(XR, 8), f4(XR + 2048, 8), dup(bb[:, 0, :], 8), dup(bb[:, 1, :], 8), pb(pwr[:, 0], 8),
                 pb(pwr[:, 1], 8), f4(HS, 8), flag="xr_ready")
            dve.wait_ge(s("xc_ready"), 8)
            stage_emptied(dve, "gate")
            link(tt(ar(IG, 4352), ar(IG, 4352), ar(XC, 4352), ALU.mult))
            dve.wait_ge(s("tanh_ready"), 4)
            link(ts(ar(HS, 4352), ar(TG, 4352), 1.0, None, ALU.add))
            link(V.reciprocal(ar(HS, 4352), ar(HS, 4352)))
            tt(ar(TG, 4352), ar(TG, 4352), ar(HS, 4352), ALU.mult).then_inc(s("ratio_ready"), 1)
            dve.wait_ge(s("root_ready"), 1)
            tt(ar(IG, 4352), ar(IG, 4352), ar(TG, 4352), ALU.mult).then_inc(s("input_ready"), 1)
            dve.wait_ge(s("input_ready"), 1)
            dve.wait_ge(s("decay_ready"), 4)
            for m in range(ML):
                o = NT * m
                V.tensor_tensor_scan(ar(HS + o, SEQ), ar(RG + o, SEQ), ar(IG + o, SEQ), 0.0, ALU.mult, ALU.add)
                link(V.tensor_tensor_scan(ar(HS + o + SEQ, DSEQ), ar(RG + o + SEQ, DSEQ), ar(IG + o + SEQ, DSEQ),
                                          par("h0")[:, m:m + 1], ALU.mult, ALU.add))
                V.tensor_copy(fin[:, 64 + m:65 + m], ar(HS + o + SEQ - 1, 1))
                last = V.tensor_copy(fin[:, 68 + m:69 + m], ar(HS + o + NT - 1, 1))
                if m == ML - 1:
                    last.then_inc(s("fin_ready"), 1)
                tk = lambda off, n: ar(off, n).rearrange("p (c k) -> p k c", k=L)
                ct = lambda off, n: ar(off, n).rearrange("p (k c) -> p k c", k=L)
                tt(ct(YL + o, SEQ), tk(HS + o, SEQ), tk(GA + o, SEQ), ALU.mult)
                last = tt(ct(YL + o + SEQ, DSEQ), tk(HS + o + SEQ, DSEQ), tk(GA + o + SEQ, DSEQ), ALU.mult)
            last.then_inc(s("yl_ready"), 1)
            dve.wait_ge(s("yl_ready"), 1)
            V.memset(ar(TT, 4096), 0.0).then_inc(s("t_zeroed"), 1)
            stage_emptied(dve, "k0")
            dd = ddg.rearrange("p (g i) -> p g i", g=G)
            link(tt(dd, dd, ident[0:GS, 0:GS].unsqueeze(1).to_broadcast([GS, G, GS]), ALU.mult))
            kb = ar(K0, 4096, GS).rearrange("p (g n) -> p g n", g=G)[:, :, 0:GS]
            tt(kb, kb, dd, ALU.add).then_inc(s("k0_ready"), 1)
            stage_emptied(dve, "ug")
            E = [ar(EE + SFLAT * r, SFLAT).rearrange("p (a n) -> p a n", a=PAIRS) for r in range(2)]
            for r, v, c in ((0, 1.0, 14), (1, 0.0, 12)):
                link(V.memset(E[r][:, :, 0:1], v))
                link(V.tensor_copy(E[r][:, :, 1], C(c)))
            for m in (1, 2, 4, 8, 16, 32, 64):
                shp = [P, PAIRS, m]
                cmul(E[0][:, :, m + 1:2 * m + 1], E[1][:, :, m + 1:2 * m + 1], E[0][:, :, 1:m + 1],
                     E[1][:, :, 1:m + 1], E[0][:, :, m:m + 1].to_broadcast(shp), E[1][:, :, m:m + 1].to_broadcast(shp),
                     ar(VV, PAIRS * m).rearrange("p (a m) -> p a m", m=m))
            for r in range(2):
                link(V.tensor_copy(E[r][:, :, NC + 1:SLOTS], E[r][:, :, 0:NCS + 1]))
            dve.wait_ge(s("toeplitz_in"), 16 * L)
            md = ar(MD, SFLAT).rearrange("p (a n) -> p a n", a=PAIRS)
            link(V.tensor_copy(md, C(4).unsqueeze(2).to_broadcast([P, PAIRS, SLOTS])))
            link(V.memset(md[:, :, 0:1], 0.0))
            link(V.memset(md[:, :, NC + 1:NC + 2], 0.0))
            vs = [ar(VV + SFLAT * r, SFLAT).rearrange("p (a n) -> p a n", a=PAIRS) for r in range(2)]
            stage_emptied(dve, "rt")
            for a in range(PAIRS):
                b = filled(dve, "v", a)
                for r in range(2):
                    V.tensor_copy(vs[r][:, a, 1:NC + 1], b[:, 136 * r:136 * r + P])
                    last = V.tensor_copy(vs[r][:, a, NC + 2:SLOTS], b[:, 136 * r + P:136 * r + 136])
                done(last)
            for r, name in enumerate(("s0re", "s0im")):
                link(V.memset(vs[r][:, :, 0:1], 0.0))
                link(V.tensor_copy(vs[r][:, :, NC + 1], par(name)))
            stage_emptied(dve, "v")
            ev, od = [ar(EE + SFLAT * r, SFLAT) for r in range(2)], [ar(VV + SFLAT * r, SFLAT) for r in range(2)]
            t1, t2 = ar(TMP, SFLAT), ar(TMP + SFLAT, SFLAT)

            tt(t1, od[0], ev[1], ALU.mult)
            link(tt(t2, od[1], ev[1], ALU.mult))
            tt(od[0], od[0], ev[0], ALU.mult)
            link(tt(od[1], od[1], ev[0], ALU.mult))
            tt(od[0], od[0], t2, ALU.add)
            link(tt(od[1], od[1], t1, ALU.subtract))
            V.tensor_tensor_scan(t1, ar(MD, SFLAT), od[0], 0.0, ALU.mult, ALU.add)
            link(V.tensor_tensor_scan(t2, ar(MD, SFLAT), od[1], 0.0, ALU.mult, ALU.add))
            tt(od[0], t1, ev[0], ALU.mult)
            tt(od[1], t1, ev[1], ALU.mult)
            link(tt(ar(MD, SFLAT), t2, ev[1], ALU.mult))
            link(tt(t2, t2, ev[0], ALU.mult))
            tt(od[0], od[0], ar(MD, SFLAT), ALU.subtract)
            tt(od[1], od[1], t2, ALU.add).then_inc(s("state_ready"), 1)
            dve.wait_ge(s("state_ready"), 1)
            for r in range(2):
                V.tensor_copy(fin[:, 16 * r:16 * r + 16], vs[r][:, :, NC])
                last = V.tensor_copy(fin[:, 32 + 16 * r:48 + 16 * r], vs[r][:, :, SLOTS - 1])
            last.then_inc(s("fin_ready"), 1)
            for j in range(4):
                for q in range(3):
                    b = filled(dve, "gyT", 3 * j + q)
                    width = 512 if q < 2 else DSEQ
                    done(V.tensor_copy(ar(GYT + NT * j + 512 * q, width), b[:, 0:width]))
            stage_emptied(dve, "glu")
            tt(ar(YS5, 4352), ar(YS5, 4352), ar(GYT, 4352), ALU.mult).then_inc(s("ys5_ready"), 1)
            dve.wait_ge(s("sq_ready"), 2)
            for src, name in ((YL, "gnl"), (YS5, "gns")):
                for m in range(ML):
                    last = ts(ar(src + NT * m, NT), ar(src + NT * m, NT), par(name)[:, m:m + 1], None, ALU.mult)
                last.then_inc(s("halves_scaled"), 1)
            b = filled(dve, "rms", 0)
            for half in range(2):
                V.tensor_copy(ssq[:, 8 * half:8 * half + 8], b[:, 9 * half:9 * half + 8])
                last = V.tensor_copy(ssq[0:DSEQ, 16 + half:17 + half], b[0:DSEQ, 9 * half + 8:9 * half + 9])
            done(last)
            stage_emptied(dve, "rms")
            rnorm(ssq[:, 0:18], ssq[:, 18:36], ssq[:, 0:18], 16, 2, DL, "ms2_ready", "rt2_ready")
            dve.wait_ge(s("x_again_in"), 32)
            for t in range(NTILE):
                n, g = cols(t)[1], t // 8
                for nh in range(2):
                    m0, m1 = ar(MT + 512 * nh, 512, n), ar(X1 + 1024 * t + 512 * nh, 512, n)
                    rl = ssq[0:n, t:t + 1] if t < 8 else ssq[0:n, 16:17]
                    rs = ssq[0:n, 8 + t:9 + t] if t < 8 else ssq[0:n, 17:18]
                    b = filled(dve, "mix", 4 * t + 2 * nh)
                    done(ts(m0, b[0:n, :], rl, None, ALU.mult))
                    dve.wait_ge(emptied["dve"], empties(where["mix", 4 * t + 2 * nh] + 1, "dve"))
                    b = filled(dve, "mix", 4 * t + 2 * nh + 1)
                    done(V.scalar_tensor_tensor(out=m0, in0=b[0:n, :], scalar=rs, in1=m0, op0=ALU.mult, op1=ALU.add))
                    dve.wait_ge(emptied["dve"], empties(where["mix", 4 * t + 2 * nh + 1] + 1, "dve"))
                    link(tt(m0, m0, ar(G1B + 1024 * g + 512 * nh, 512, n), ALU.mult))
                    last = tt(m1, m1, m0, ALU.add)
                    if nh == 0:
                        link(last)
                last.then_inc(s("x1_ready"), 1)
            dve.wait_ge(s("ssq3"), NTILE)
            rnorm(rms3[:, 0:9], rms3[:, 10:19], rms3[:, 20:29], 8, 1, DM, "ms3_ready", "rt3_ready")
            for t in range(NTILE):
                n = cols(t)[1]
                ts(ar(XN2 + 1024 * t, 1024, n), ar(X1 + 1024 * t, 1024, n), rms3[0:n, 20 + t:21 + t], None,
                   ALU.mult).then_inc(s("xn2_ready"), 1)
            dve.wait_ge(s("a2_ready"), 1)
            modulated(dve, "dve", "h2T", h2_buf, a2, 24)
            stage_emptied(dve, "h2T")
            dve.wait_ge(s("x1_out"), 32)

            def head_picks(h, first=False, last_head=False):
                cnt = [0]

                def lk(ins):
                    cnt[0] += 1
                    ins.then_inc(s("pick_chain"), 1)
                    dve.wait_ge(s("pick_chain"), NLINK * h + cnt[0])

                def top16(scores, width, vals, idx):
                    rest = lambda t, n: ar(CW2 + width * t, width, n)
                    for half, src in ((0, scores), (1, rest)):
                        e = slice(8 * half, 8 * half + 8)
                        V.memset(mark[:, 0:1], 0.0)
                        for t in range(NTILE):
                            n = cols(t)[1]
                            last = V.max(vals[0:n, t, e], src(t, n))
                        lk(last)
                        V.memset(mark[:, 0:1], 0.0)
                        for t in range(NTILE):
                            n = cols(t)[1]
                            last = V.max_index(idx[0:n, t, e], vals[0:n, t, e], src(t, n))
                            if half == 0:
                                last = V.match_replace(rest(t, n), vals[0:n, t, e], src(t, n), NEG)
                        lk(last)

                for c in range(2):
                    dve.wait_ge(s("s_moved"), 2 * h + c + 1)
                    top16(lambda t, n: ar(SB + 1152 * c + P * t, P, n), P, vtop[:, c], itop[:, c])
                    V.memset(mark[:, 1 + c:2 + c], 0.0).then_inc(s("scores_read"), 1)
                for n, t0, nt in ((P, 0, 8), (DSEQ, 8, 1)):
                    rows = ar(CAND + NCAND * t0, NCAND * nt, n).rearrange("p (t x) -> p t x", t=nt)
                    for at, a0, na, nb in ((0, 0, 4, TOPK), (64, 4, TOPK - 4, 4)):
                        last = tt(rows[:, :, at:at + na * nb].rearrange("p t (a b) -> p t a b", a=na),
                                  vtop[0:n, 0, t0:t0 + nt, a0:a0 + na].unsqueeze(3).to_broadcast([n, nt, na, nb]),
                                  vtop[0:n, 1, t0:t0 + nt, 0:nb].unsqueeze(2).to_broadcast([n, nt, na, nb]), ALU.add)
                lk(last)
                top16(lambda t, n: ar(CAND + NCAND * t, NCAND, n), NCAND, smx, pos)
                for n, t0, nt in ((P, 0, 8), (DSEQ, 8, 1)):
                    last = V.tensor_copy(mx1[0:n, t0:t0 + nt, :], smx[0:n, t0:t0 + nt, 0:1])
                lk(last)
                for n, t0, nt in ((P, 0, 8), (DSEQ, 8, 1)):
                    v = smx[0:n, t0:t0 + nt, :]
                    last = tt(v, v, mx1[0:n, t0:t0 + nt, :].to_broadcast([n, nt, TOPK]), ALU.subtract)
                last.then_inc(s("softmax_in"), 1)
                if not first:
                    dve.wait_ge(s("decoded"), h)
                for n, t0, nt in ((P, 0, 8), (DSEQ, 8, 1)):
                    V.tensor_copy(itf[0:n, :, t0:t0 + nt, :], itop[0:n, :, t0:t0 + nt, :])
                    pv = pos[0:n, t0:t0 + nt, :]
                    ts(posab[0:n, 0, t0:t0 + nt, :], pv, 4, None, ALU.logical_shift_right)
                    ts(quad[0:n, t0:t0 + nt, :], pv, 2, None, ALU.logical_shift_right)
                    last = ts(posab[0:n, 1, t0:t0 + nt, :], pv, 64.0, 12.0, ALU.is_lt, ALU.mult)
                lk(last)
                for n, t0, nt in ((P, 0, 8), (DSEQ, 8, 1)):
                    V.scalar_tensor_tensor(out=pf[0:n, 0, t0:t0 + nt, :], in0=quad[0:n, t0:t0 + nt, :], scalar=-12.0,
                                           in1=posab[0:n, 0, t0:t0 + nt, :], op0=ALU.add, op1=ALU.max)
                    last = ts(posab[0:n, 1, t0:t0 + nt, :], posab[0:n, 1, t0:t0 + nt, :], 3, None, ALU.bitwise_or)
                lk(last)
                for n, t0, nt in ((P, 0, 8), (DSEQ, 8, 1)):
                    last = tt(posab[0:n, 1, t0:t0 + nt, :], posab[0:n, 1, t0:t0 + nt, :], pos[0:n, t0:t0 + nt, :],
                              ALU.bitwise_and)
                lk(last)
                for n, t0, nt in ((P, 0, 8), (DSEQ, 8, 1)):
                    last = V.tensor_copy(pf[0:n, 1, t0:t0 + nt, :], posab[0:n, 1, t0:t0 + nt, :])
                lk(last)
                for n, t0, nt in ((P, 0, 8), (DSEQ, 8, 1)):
                    shp = [n, nt, TOPK, TOPK]
                    last = tt(ar(D0 + 256 * t0, 256 * nt, n).rearrange("p (t j a) -> p t j a", t=nt, j=TOPK),
                              pf[0:n, 0, t0:t0 + nt, :].unsqueeze(3).to_broadcast(shp),
                              iota[0:n, 0:TOPK].unsqueeze(1).unsqueeze(1).to_broadcast(shp), ALU.is_equal)
                if not last_head:
                    last.then_inc(s("positions_ready"), 1)
                if last_head:
                    for n, t0, nt in ((P, 0, 8), (DSEQ, 8, 1)):
                        shp = [n, nt, TOPK, TOPK]
                        last = tt(ar(CAND + 256 * t0, 256 * nt, n).rearrange("p (t j a) -> p t j a", t=nt, j=TOPK),
                                  pf[0:n, 1, t0:t0 + nt, :].unsqueeze(3).to_broadcast(shp),
                                  iota[0:n, 0:TOPK].unsqueeze(1).unsqueeze(1).to_broadcast(shp), ALU.is_equal)
                    lk(last)
                    both = [(c, off, n, t0, nt) for c, off in ((0, D0), (1, CAND))
                            for n, t0, nt in ((P, 0, 8), (DSEQ, 8, 1))]
                    for c, off, n, t0, nt in both:
                        v4 = ar(off + 256 * t0, 256 * nt, n).rearrange("p (t j a) -> p t j a", t=nt, j=TOPK)
                        last = tt(v4, v4, itf[0:n, c, t0:t0 + nt, :].unsqueeze(2).to_broadcast(
                            [n, nt, TOPK, TOPK]), ALU.mult)
                    lk(last)
                    for c, off, n, t0, nt in both:
                        v4 = ar(off + 256 * t0, 256 * nt, n).rearrange("p (t j a) -> p t j a", t=nt, j=TOPK)
                        last = V.tensor_reduce(iall(c, n, t0, nt, h), v4, AX.X, ALU.add)
                    lk(last)
                dve.wait_ge(s("softmax_exp"), h + 1)
                for n, t0, nt in ((P, 0, 8), (DSEQ, 8, 1)):
                    last = V.tensor_reduce(mx1[0:n, t0:t0 + nt, :].rearrange("p t o -> p (t o)"),
                                           smx[0:n, t0:t0 + nt, :], AX.X, ALU.add)
                lk(last)
                for n, t0, nt in ((P, 0, 8), (DSEQ, 8, 1)):
                    last = V.reciprocal(mx1[0:n, t0:t0 + nt, :], mx1[0:n, t0:t0 + nt, :])
                lk(last)
                for n, t0, nt in ((P, 0, 8), (DSEQ, 8, 1)):
                    last = tt(iall(2, n, t0, nt, h), smx[0:n, t0:t0 + nt, :],
                              mx1[0:n, t0:t0 + nt, :].to_broadcast([n, nt, TOPK]), ALU.mult)
                last.then_inc(s("picks_ready"), 1)
                dve.wait_ge(s("picks_ready"), h + 1)
                return cnt[0]

            head_picks(0, True)
            with dve.Fori(1, HEADS - 1) as h:
                got = head_picks(h)
            head_picks(HEADS - 1, last_head=True)
            assert got == NLINK, got

            dve.wait_ge(s("q_full"), 2 * HEADS)
            dve.wait_ge(s("h_split"), 1)
            tt(h_lo[:, :], seg(h2_buf, 0, 8704), h_hi[:, :].bitcast(F32), ALU.subtract).then_inc(s("h_split"), 1)
            dve.wait_ge(s("picksT_moved"), 9)

            def onehots(b, first):
                for g in range(8):
                    if not (first and g < 4):
                        dve.wait_ge(s("c_full"), 8 * b + g - 3)
                    shp = [P, 2, 8, P]
                    both = ar(ITR, 2 * NT).rearrange("p (a n) -> p a n", a=2)[:, :, bass.ds(64 * b + 8 * g, 8)]
                    tt(ar(PQ + 2048 * (g % 4), 2048).rearrange("p (a j n) -> p a j n", a=2, j=8),
                       iota[:, :].unsqueeze(1).unsqueeze(1).to_broadcast(shp),
                       both.unsqueeze(3).to_broadcast(shp), ALU.is_equal).then_inc(s("onehots_ready"), 1)

            onehots(0, True)
            onehots(1, False)
            with dve.Fori(1, 8) as i:
                onehots(2 * i, False)
                onehots(2 * i + 1, False)
            onehots(16, False)
            dve.wait_ge(s("coef_out0"), 16 * 9)
            dve.wait_ge(s("coef_out1"), 16 * 8)
            V.memset(seg(y_sum_buf, 0, 8704), 0.0).then_inc(s("y_clear"), 1)
            dve.wait_ge(s("y_clear"), 1)

            def weigh(t, u):
                for j in range(7):
                    if j == 0:
                        dve.wait_ge(s("c_in"), 16 * t + 16)
                    if j < 6:
                        k0, nk, width = CHUNKS[j % 3]
                        dve.wait_ge(s("s_gelu"), 6 * t + j + 1)
                        w = seg(w_in_buf, 2176 * u + NT * (j // 3) + P * k0, width).rearrange("p (b n) -> p b n", n=64)
                        c = seg(c_in_buf, 0, 2176).rearrange("p (b e n) -> p b e n", b=17, e=2)[
                            :, 2 * k0:2 * k0 + width // 64, j // 3, :]
                        tt(w, w, c, ALU.mult).then_inc(s("w_weighed"), 1)
                    if j > 0:
                        k0, nk, width = CHUNKS[(j - 1) % 3]
                        o = 2176 * u + NT * ((j - 1) // 3) + P * k0
                        dve.wait_ge(s("w_hi_ready"), 6 * t + j)
                        tt(w_lo[:, o:o + width], seg(w_in_buf, o, width), w_hi[:, o:o + width].bitcast(F32),
                           ALU.subtract).then_inc(s("w_lo_ready"), 1)

            def add_up(t, first):
                if not first:
                    dve.wait_ge(s("y_added"), 24 * t)
                for d in range(8):
                    for q, (k0, nk, width) in enumerate(CHUNKS):
                        j = 3 * d + q
                        dve.wait_ge(s("v_bank_full"), 24 * t + j + 1)
                        y = seg(y_sum_buf, NT * d + P * k0, width)
                        tt(y, ps[4 + j % 4][:, 0:width], y, ALU.add).then_inc(s("y_added"), 1)

            weigh(0, 0)
            weigh(1, 1)
            add_up(0, True)
            with dve.Fori(1, 32) as i:
                weigh(2 * i, 0)
                add_up(2 * i - 1, False)
                weigh(2 * i + 1, 1)
                add_up(2 * i, False)
            add_up(63, False)
            dve.wait_ge(s("y_added"), 24 * 64)
            for d in range(8):
                ts(seg(y_sum_buf, NT * d, SEQ), seg(y_sum_buf, NT * d, SEQ), mcol[:, 40 + d, 0:1], None, ALU.mult)
                last = ts(seg(y_sum_buf, NT * d + SEQ, DSEQ), seg(y_sum_buf, NT * d + SEQ, DSEQ), mcol[:, 40 + d, 1:2], None, ALU.mult)
            last.then_inc(s("y_scaled"), 1)
            dve.wait_ge(s("x1_back"), 32)
            for t in range(NTILE):
                n = cols(t)[1]
                dve.wait_ge(s("yT_full"), t + 1)
                for half in range(2):
                    x = seg(x1_buf, 1024 * t + 512 * half, 512, n)
                    last = tt(x, ps[2 * (t % 4) + half][0:n, :], x, ALU.add)
                    if half == 0:
                        link(last)
                last.then_inc(s("x2_done"), 1)
            dve.wait_ge(s("ssq4"), NTILE)
            rnorm(rms4[:, 0:9], rms4[:, 10:19], rms4[:, 20:29], 8, 1, DM, "ms4_ready", "rt4_ready")
            dve.wait_ge(s("norm_f_in"), 16)
            for t in range(NTILE):
                n = cols(t)[1]
                x = seg(x1_buf, 1024 * t, 1024, n)
                V.scalar_tensor_tensor(out=x, in0=x, scalar=rms4[0:n, 20 + t:21 + t], in1=seg(norm_f_buf, 0, 1024, n),
                                       op0=ALU.mult, op1=ALU.mult).then_inc(s("y_ready"), 1)


_ROWS = {"pack": (P, NPACK), "b_ada": (2, 6 * DM), "ddiag": (GS, DL), "w_ada": (DM, 6 * DM), "xp": (P, L, DM),
         "xs": (DSEQ, DM), "w_in": (DM, DIN), "w_glu": (DL, DL), "w_out": (DM, DM), "keys": (P, 2048),
         "wq": (HEADS, P, 2048), "ut": (P, P, DM), "vt": (64, P, 2048), "norm_f": (P, DM)}
_OUTS = {"yp": (P, L, DM), "ys": (DSEQ, DM), "conv_p": (P, ML, 3), "conv_s": (P, ML, 3), "fin": (P, 72)}


def kernel(**inputs):
    import numpy as np
    import concourse.bacc as bacc
    from concourse.bass_utils import run_bass_kernel_spmd as run

    v = {k: np.asarray(a) for k, a in inputs.items()}

    def chan(a):
        return a.reshape(a.shape[0], -1, P).transpose(2, 1, 0)

    def pairs(a):
        a = a.reshape((PAIRS, 2, SP) + a.shape[2:])
        return np.moveaxis(a, 0, 2).reshape((P, PAIRS) + a.shape[3:])

    def heads(a):
        out = np.zeros((P, ML, P), a.dtype)
        for h in range(8):
            o = 64 * (h % 2)
            out[o:o + 64, h // 2, o:o + 64] = a[h]
        return out

    cols = {
        "cT": chan(np.concatenate([v["c_prompt"], v["c_sample"]])), "norm1": chan(v["norm1"]),
        "norm2": chan(v["norm2"]), "conv_w": chan(v["conv_w"][0]), "conv_b": chan(v["conv_b"]),
        "ba": chan(v["lru_ba"]), "bx": chan(v["lru_bx"]), "lam": chan(v["lru_lam"]), "bglu": chan(v["s5_b_glu"]),
        "gnl": chan(v["gn_lru"]), "gns": chan(v["gn_s5"]), "h0": chan(v["state_lru"][0]),
        "cache": chan(v["cache_conv"][0, 0]), "are": pairs(v["s5_a_re"][0]), "aim": pairs(v["s5_a_im"][0]),
        "ldt": pairs(np.broadcast_to(v["s5_log_dt"][0][:, None], (G, SP))),
        "s0re": pairs(v["state_s5_re"][0, 0]), "s0im": pairs(v["state_s5_im"][0, 0]),
        "bre": pairs(v["s5_b_re"][0]), "bim": pairs(v["s5_b_im"][0]),
        "cre": pairs(v["s5_c_re"][0].transpose(0, 2, 1)), "cim": pairs(v["s5_c_im"][0].transpose(0, 2, 1)),
        "wa": heads(v["lru_wa"][0]), "wx": heads(v["lru_wx"][0]),
    }
    data = {
        "pack": np.concatenate([cols[n].reshape(P, -1) for n in PACK], axis=1),
        "b_ada": np.broadcast_to(v["b_ada"], (2, 6 * DM)),
        "ddiag": np.broadcast_to(v["s5_d"], (GS, DL)),
        "w_ada": v["w_ada"][0],
        "xp": v["x_prompt"][0].reshape(P, L, DM),
        "xs": v["x_sample"][0].reshape(NCS, L, DM).transpose(1, 0, 2).reshape(DSEQ, DM),
        "w_in": v["w_in"][0], "w_glu": v["s5_w_glu"][0], "w_out": v["w_out"][0],
        "keys": v["peer_keys"][0].transpose(3, 0, 1, 2).reshape(P, 2048),
        "wq": v["peer_wq"][0].reshape(DK, P, HEADS, 2, P).transpose(2, 1, 3, 0, 4).reshape(HEADS, P, 2048),
        "ut": v["peer_u"][0].reshape(P, P, DK, P).transpose(1, 3, 2, 0).reshape(P, P, DM),
        "vt": v["peer_v"][0].reshape(P, 64, 2, DM).transpose(1, 0, 2, 3).reshape(64, P, 2048),
        "norm_f": np.broadcast_to(v["norm_f"], (P, DM)),
    }
    nc = bacc.Bacc("TRN2", target_bir_lowering=False, num_devices=1)
    A, O, arrays = {}, {}, {}
    for name, shape in _ROWS.items():
        arrays[f"in_{name}"] = np.ascontiguousarray(data[name])
        assert arrays[f"in_{name}"].shape == shape, (name, arrays[f"in_{name}"].shape)
        A[name] = nc.dram_tensor(f"in_{name}", shape, F32, kind="ExternalInput").ap()
    for name, shape in _OUTS.items():
        O[name] = nc.dram_tensor(f"out_{name}", shape, F32, kind="ExternalOutput").ap()
    trunk(nc, A, O)
    r = run(nc, [arrays], core_ids=[0]).results[0]
    yp = r["out_yp"].reshape(1, SEQ, DM)
    ys = r["out_ys"].reshape(L, NCS, DM).transpose(1, 0, 2).reshape(1, DSEQ, DM)
    conv = [r[f"out_{n}"].transpose(2, 1, 0).reshape(1, 1, 3, DL) for n in ("conv_p", "conv_s")]
    f = r["out_fin"]

    def s5(o):
        return f[:, o:o + 16].reshape(2, SP, PAIRS).transpose(2, 0, 1).reshape(1, 1, G, SP)

    lru = [f[:, o:o + 4].T.reshape(1, 1, DL) for o in (64, 68)]
    return tuple(np.ascontiguousarray(a) for a in
                 (yp, ys, conv[0], lru[0], s5(0), s5(16), conv[1], lru[1], s5(32), s5(48)))
```
